# Optimizing a Trainium2 kernel written in Bass

```python
import math
import jax, jax.numpy as jnp
from jax import lax
import numpy as np

D_MODEL = 1024
BATCH = 1
SEQ = 1024
DEPTH = 1

D_MIX = D_MODEL
D_ATTN = D_MIX // 2
D_POOL = D_MIX - D_ATTN
N_DIFF_HEADS = 4
DIFF_QK_DIM = D_ATTN // (2 * N_DIFF_HEADS)
DIFF_V_DIM = 2 * DIFF_QK_DIM
POOL_WINDOWS = (2, 4, 8, 16)
N_POOL_GROUPS = len(POOL_WINDOWS)
POOL_GROUP_DIM = D_POOL // N_POOL_GROUPS
D_IN_PROJ = 3 * D_ATTN + D_POOL
N_EXPERTS = 32
TOP_K = 4
D_FF = D_MODEL
SWIGLU_LIMIT = 7.0
SWIGLU_ALPHA = 1.702
Q_BLOCK = 128
MOE_BLOCK = 128
RMS_EPS = 1e-5

kernel_name = "hymba_style_diffattn_pool_moe_block"

def rmsnorm(x, g):
    xf = x.astype(jnp.float32)
    y = xf * lax.rsqrt(jnp.mean(xf * xf, axis=-1, keepdims=True) + RMS_EPS)
    return (y * g.astype(jnp.float32)).astype(x.dtype)

def diff_attention(q, k, v, lam, subln_g, lambda_init):
    B, S, H, _, DK = q.shape
    nb = S // Q_BLOCK
    qb = jnp.moveaxis(q.reshape(B, nb, Q_BLOCK, H, 2, DK), 1, 0)
    key_pos = jnp.arange(S)
    scale = DK ** -0.5

    def one_block(args):
        i, q_i = args
        q_pos = i * Q_BLOCK + jnp.arange(Q_BLOCK)
        s = jnp.einsum('bqhmd,bkhmd->bhmqk', q_i, k,
                       preferred_element_type=jnp.float32) * scale
        causal = key_pos[None, :] <= q_pos[:, None]
        s = jnp.where(causal, s, -jnp.inf)
        p = jax.nn.softmax(s, axis=-1)
        a = p[:, :, 0] - lam * p[:, :, 1]
        return jnp.einsum('bhqk,bkhd->bqhd', a.astype(v.dtype), v)

    o = lax.map(one_block, (jnp.arange(nb), qb))
    o = jnp.moveaxis(o, 0, 1).reshape(B, S, H, DIFF_V_DIM)
    o = rmsnorm(o, subln_g) * (1.0 - lambda_init)
    return o.reshape(B, S, H * DIFF_V_DIM)

def multiscale_pool(u, w_pool, b_pool, pool_scale):
    B, S, _ = u.shape
    uf = u.astype(jnp.float32).reshape(B, S, N_POOL_GROUPS, POOL_GROUP_DIM)
    csum = jnp.cumsum(uf, axis=1)
    pos1 = jnp.arange(1, S + 1)
    outs = []
    for g, w in enumerate(POOL_WINDOWS):
        c = csum[:, :, g]
        c_prev = jnp.pad(c, ((0, 0), (w, 0), (0, 0)))[:, :S]
        cnt = jnp.minimum(pos1, w).astype(jnp.float32)[None, :, None]
        outs.append((c - c_prev) / cnt - uf[:, :, g])
    z = jnp.stack(outs, axis=2).astype(u.dtype)
    y = jnp.einsum('bsgc,gcd->bsgd', z, w_pool) + b_pool
    return y.reshape(B, S, D_POOL) * pool_scale

def moe(h, router_w, router_b, w_gate, b_gate, w_up, b_up, w_down, b_down):
    T = h.shape[0]
    logits = (h @ router_w + router_b).astype(jnp.float32)
    top_vals, top_idx = lax.top_k(logits, TOP_K)
    gates = jax.nn.softmax(top_vals, axis=-1)
    A = T * TOP_K
    flat_e = top_idx.reshape(A)
    flat_tok = jnp.arange(A, dtype=jnp.int32) // TOP_K
    flat_g = gates.reshape(A)
    order = jnp.argsort(flat_e)
    sorted_e = flat_e[order]
    counts = jnp.bincount(flat_e, length=N_EXPERTS)
    padded = ((counts + MOE_BLOCK - 1) // MOE_BLOCK) * MOE_BLOCK
    group_start = jnp.cumsum(counts) - counts
    padded_end = jnp.cumsum(padded)
    padded_start = padded_end - padded
    dest = padded_start[sorted_e] + (jnp.arange(A) - group_start[sorted_e])
    n_blocks = (A + N_EXPERTS * (MOE_BLOCK - 1) + MOE_BLOCK - 1) // MOE_BLOCK
    P = n_blocks * MOE_BLOCK
    slot_tok = jnp.zeros((P,), jnp.int32).at[dest].set(flat_tok[order])
    slot_gate = jnp.zeros((P,), jnp.float32).at[dest].set(flat_g[order])
    block_expert = jnp.clip(
        jnp.searchsorted(padded_end, jnp.arange(n_blocks) * MOE_BLOCK, side='right'),
        0, N_EXPERTS - 1)

    def expert_block(args):
        e, tok, g = args
        xb = h[tok]
        gate = jnp.minimum(xb @ w_gate[e] + b_gate[e], SWIGLU_LIMIT)
        up = jnp.clip(xb @ w_up[e] + b_up[e], -SWIGLU_LIMIT, SWIGLU_LIMIT)
        act = gate * jax.nn.sigmoid(SWIGLU_ALPHA * gate) * (up + 1.0)
        y = act @ w_down[e] + b_down[e]
        return y * g.astype(y.dtype)[:, None]

    ys = lax.map(expert_block, (block_expert,
                                slot_tok.reshape(n_blocks, MOE_BLOCK),
                                slot_gate.reshape(n_blocks, MOE_BLOCK)))
    return jnp.zeros_like(h).at[slot_tok].add(ys.reshape(P, h.shape[1]))

def setup_inputs(seed: int = 0) -> dict:
    key = jax.random.key(seed)
    ks = jax.random.split(key, 24)
    f32 = jnp.float32
    L = DEPTH

    def nrm(k, shape, scale):
        return jax.random.normal(k, shape, f32) * scale

    return {
        "x": nrm(ks[0], (BATCH, SEQ, D_MODEL), 1.0),
        "norm1_g": 1.0 + nrm(ks[1], (L, D_MODEL), 0.02),
        "w_in": nrm(ks[2], (L, D_MODEL, D_IN_PROJ), D_MODEL ** -0.5),
        "lambda_q1": nrm(ks[3], (L, DIFF_QK_DIM), 0.1),
        "lambda_k1": nrm(ks[4], (L, DIFF_QK_DIM), 0.1),
        "lambda_q2": nrm(ks[5], (L, DIFF_QK_DIM), 0.1),
        "lambda_k2": nrm(ks[6], (L, DIFF_QK_DIM), 0.1),
        "subln_g": 1.0 + nrm(ks[7], (L, DIFF_V_DIM), 0.02),
        "w_pool": nrm(ks[8], (L, N_POOL_GROUPS, POOL_GROUP_DIM, POOL_GROUP_DIM), POOL_GROUP_DIM ** -0.5),
        "b_pool": nrm(ks[9], (L, N_POOL_GROUPS, POOL_GROUP_DIM), 0.01),
        "pool_scale": 1.0 + nrm(ks[10], (L, D_POOL), 0.02),
        "w_out": nrm(ks[11], (L, D_MIX, D_MODEL), D_MIX ** -0.5),
        "norm2_g": 1.0 + nrm(ks[12], (L, D_MODEL), 0.02),
        "router_w": nrm(ks[13], (L, D_MODEL, N_EXPERTS), D_MODEL ** -0.5),
        "router_b": nrm(ks[14], (L, N_EXPERTS), 0.01),
        "w_gate": nrm(ks[15], (L, N_EXPERTS, D_MODEL, D_FF), D_MODEL ** -0.5),
        "b_gate": nrm(ks[16], (L, N_EXPERTS, D_FF), 0.01),
        "w_up": nrm(ks[17], (L, N_EXPERTS, D_MODEL, D_FF), D_MODEL ** -0.5),
        "b_up": nrm(ks[18], (L, N_EXPERTS, D_FF), 0.01),
        "w_down": nrm(ks[19], (L, N_EXPERTS, D_FF, D_MODEL), D_FF ** -0.5),
        "b_down": nrm(ks[20], (L, N_EXPERTS, D_MODEL), 0.01),
        "final_g": 1.0 + nrm(ks[21], (D_MODEL,), 0.02),
    }

def reference(x, norm1_g, w_in, lambda_q1, lambda_k1, lambda_q2, lambda_k2, subln_g,
              w_pool, b_pool, pool_scale, w_out, norm2_g, router_w, router_b,
              w_gate, b_gate, w_up, b_up, w_down, b_down, final_g):
    B, S, D = x.shape
    for l in range(DEPTH):
        lambda_init = 0.8 - 0.6 * math.exp(-0.3 * l)
        lam = (jnp.exp(jnp.sum(lambda_q1[l].astype(jnp.float32) * lambda_k1[l].astype(jnp.float32)))
               - jnp.exp(jnp.sum(lambda_q2[l].astype(jnp.float32) * lambda_k2[l].astype(jnp.float32)))
               + lambda_init)
        h = rmsnorm(x, norm1_g[l])
        proj = h @ w_in[l]
        q, k, v, u = jnp.split(proj, [D_ATTN, 2 * D_ATTN, 3 * D_ATTN], axis=-1)
        q = q.reshape(B, S, N_DIFF_HEADS, 2, DIFF_QK_DIM)
        k = k.reshape(B, S, N_DIFF_HEADS, 2, DIFF_QK_DIM)
        v = v.reshape(B, S, N_DIFF_HEADS, DIFF_V_DIM)
        attn_out = diff_attention(q, k, v, lam, subln_g[l], lambda_init)
        pool_out = multiscale_pool(u, w_pool[l], b_pool[l], pool_scale[l])
        x = x + jnp.concatenate([attn_out, pool_out], axis=-1) @ w_out[l]
        h = rmsnorm(x, norm2_g[l])
        y = moe(h.reshape(B * S, D), router_w[l], router_b[l], w_gate[l], b_gate[l],
                w_up[l], b_up[l], w_down[l], b_down[l])
        x = x + y.reshape(B, S, D)
    return rmsnorm(x, final_g)


_drawn_inputs = setup_inputs


def setup_inputs(seed=0):
    import zlib

    import numpy as np

    out = dict(_drawn_inputs(seed))
    spreads = {}
    factors = {'lambda_q2': 34.365,
     'b_gate': 8.0,
     'b_up': 22.425,
     'b_down': 8.0,
     'final_g': 7.554,
     'b_pool': 2.893}
    for name, (base, spread) in spreads.items():
        noise = np.random.default_rng([zlib.crc32(name.encode()), seed]).standard_normal(out[name].shape)
        drawn = base * np.exp(spread * noise) if base else spread * noise
        out[name] = __import__('jax').numpy.asarray(drawn.astype(out[name].dtype))
    for name, factor in factors.items():
        out[name] = (out[name] * factor).astype(out[name].dtype)
    return out
```

```python
import numpy as np
import concourse.bass as bass
import concourse.mybir as mybir
from concourse.alu_op_type import AluOpType as ALU
from contextlib import ExitStack

ACT = mybir.ActivationFunctionType
AX = mybir.AxisListType.X
F32, F32R, I32, U32 = mybir.dt.float32, mybir.dt.float32r, mybir.dt.int32, mybir.dt.uint32

P = 128
S, D = 1024, 1024
TB, KC = S // P, D // P
D_ATTN, HEADS, DQK, DV = 512, 4, 64, 128
POOLS = 4
WMAX = 2 ** POOLS
LAMBDA_INIT = 0.8 - 0.6
EPS = 1e-5
E, TOPK = 32, 4
LIMIT, ALPHA = 7.0, 1.702
HALF = 512
SLOTS = 256
ITEMS = (S * TOPK + E * (SLOTS - 1)) // SLOTS
LEVELS = (96, 128, 160, 192, 256)
ROWS = S + SLOTS
GROUPS = 6
MASKED = -1e30
MAGIC = 0x5F3759DF


class Order:

    def __init__(self, eng, sem, base=0):
        self.eng, self.sem, self.n, self.base = eng, sem, 0, base

    def did(self, ins):
        self.n += 1
        ins.then_inc(self.sem, 1)

    def need(self):
        if isinstance(self.base, int) and not self.base + self.n:
            return
        self.eng.wait_ge(self.sem, self.base + self.n)


def bcast(ap, n):
    return ap.unsqueeze(2).broadcast_to([ap.shape[0], ap.shape[1], n])


def repeat(ap, n):
    return ap.unsqueeze(1).broadcast_to([ap.shape[0], n, ap.shape[1]])


def rsqrt_mean(eng, order, out, sums, tmp, n, extra=1.0):
    v, t, y = tmp[:, 0], tmp[:, 1], tmp[:, 2]
    order.need()
    order.did(eng.tensor_scalar(v, sums, 1.0 / n, EPS, ALU.mult, ALU.add))
    order.need()
    order.did(eng.tensor_scalar(t.bitcast(I32), v.bitcast(I32), 1, None, ALU.logical_shift_right))
    order.need()
    order.did(eng.tensor_scalar(y.bitcast(I32), t.bitcast(I32), -1.0, float(MAGIC), ALU.mult, ALU.add))
    for step in range(4):
        order.need()
        order.did(eng.tensor_tensor(t, y, y, ALU.mult))
        order.need()
        order.did(eng.tensor_tensor(t, t, v, ALU.mult))
        order.need()
        order.did(eng.tensor_scalar(t, t, -0.5, 1.5, ALU.mult, ALU.add))
        order.need()
        order.did(eng.tensor_tensor(y, y, t, ALU.mult))
    order.need()
    order.did(eng.tensor_scalar(out, y, float(extra), None, ALU.mult))


def mixer(nc, d, keep, rows):
    with ExitStack() as ctx:
        sb = lambda name, shape, dt=F32: ctx.enter_context(nc.sbuf_tensor(name, shape, dt))
        sem = lambda name: ctx.enter_context(nc.semaphore(name))
        ps = ctx.enter_context(nc.psum_tensor("ps_mixer", [P, 8, HALF], F32))
        x = sb("x", [P, TB, D])
        xn = sb("xn", [P, TB, D])
        hT = sb("hT", [P, KC, S])
        qkT = sb("qkT", [P, 2, HEADS, S])
        v = sb("v", [P, TB, D_ATTN])
        uT = sb("uT", [P, POOLS, S])
        ring = sb("w_ring", [P, 2, KC, HALF])
        g2 = sb("g2", [P, D])
        mask = sb("mask", [P, P])
        wp = sb("wp", [P, POOLS, P])
        rw = sb("rw", [P, KC, E])
        rb = sb("rb", [P, E])
        vec_rows = sb("vec_rows", [17, P])
        vec = sb("vec", [P, 17])
        lam_in = sb("lam_in", [P, 4, DQK])
        lam = sb("lam", [P, 8])
        ss = sb("ss", [P, TB])
        rstd = sb("rstd", [P, TB])
        tmp = sb("tmp", [P, 3, TB])
        inv_i = sb("inv_i", [P, WMAX], I32)
        inv = sb("inv", [P, 5, WMAX])
        soft = sb("soft", [P, 8, 2])
        r0 = sb("r0", [P, 2, HEADS])
        ident = keep.ident
        junk = uT[:, 3]
        pool_a, pool_b = xn[:, 0], xn[:, 1]
        probs = xn[:, 2:6]
        comb = xn[:, 6:8]
        combT = xn[:, 1].rearrange("p (k t) -> p k t", t=P)
        ot = xn[:, 0, HALF:D]
        mixT, h2T = hT, qkT.rearrange("p a h s -> p (a h) s")
        g_in = vec[:, 0:8]
        b_pool, s_pool, g_sub = vec[:, 8:12], vec[:, 12:16], vec[:, 16:17]

        x_in = [sem(f"x_in{b}") for b in range(TB)]
        vec_in, lam_ld, g2_in, wp_in, rw_in, rb_in = (sem(n) for n in ("vec_in", "lam_ld", "g2_in", "wp_in", "rw_in", "rb_in"))
        w_in = [sem(f"w_in{i}") for i in range(6)]
        zeroed, zero_st = sem("zeroed"), [sem(f"zero_st{i}") for i in range(4)]
        consts, squares, normed, vec_ready = sem("consts"), sem("squares"), sem("normed"), sem("vec_ready")
        vec_mm, job_done, lam_exp = sem("vec_mm"), sem("job_done"), sem("lam_exp")
        ev = {"act": sem("ev_act"), "dve": sem("ev_dve")}
        order_s, pool_s, lam_s = sem("order_s"), sem("pool_s"), sem("lam_s")
        pooled = sem("pooled")
        scored, biased, exped, combined = sem("scored"), sem("biased"), sem("exped"), sem("combined")
        turned, turn_ev, o_done, o_norm, oT_done, mixed = (sem(n) for n in ("turned", "turn_ev", "o_done", "o_norm", "oT_done", "mixed"))
        x1_ready, h2_ready, sq2, router_mm, router_ev = (sem(n) for n in ("x1_ready", "h2_ready", "sq2", "router_mm", "router_ev"))
        st = [sem(f"st{i}") for i in range(2 * TB)]

        jobs = [("norm", q, k, "act" if k % 2 else "dve") for q in range(2) for k in range(KC)]
        jobs += [(w, h, q, "act" if q else "dve") for w in ("q", "k", "u") for h in range(4) for q in range(2)]
        jobs += [("v", b, 0, "act") for b in range(TB)]
        jobs += [("pool", g, q, "dve") for g in range(POOLS) for q in range(2)]
        first_out = len(jobs)
        jobs += [("out", b, n, "dve") for b in range(TB) for n in range(2)]
        jobs += [("norm2", q, k, "act" if k % 2 else "dve") for q in range(2) for k in range(KC)]
        tile_of = {"q": 0, "k": 1, "u": 2, "v": 3}

        def emptied(n):
            who = jobs[n][3]
            return who, sum(j[3] == who for j in jobs[:n + 1])

        units = [(i, h) for i in range(TB) for h in range(HEADS)]

        with nc.Block() as block:

            @block.sync
            def _(sp):
                sp.dma_start(vec_rows[0:8, :], d["norm1_g"].rearrange("a (k p) -> (a k) p", p=P)).then_inc(vec_in, 16)
                sp.dma_start(vec_rows[8:12, :], d["b_pool"].rearrange("a g p -> (a g) p")).then_inc(vec_in, 16)
                sp.dma_start(vec_rows[12:16, :], d["pool_scale"].rearrange("a (g p) -> (a g) p", p=P)).then_inc(vec_in, 16)
                sp.dma_start(vec_rows[16:17, :], d["subln_g"]).then_inc(vec_in, 16)
                for b in range(TB):
                    sp.dma_start(x[:, b, :], d["x"][0, b * P:(b + 1) * P, :]).then_inc(x_in[b], 16)
                for t, c in enumerate((0, 1, 3, 2)):
                    if t >= 2:
                        sp.wait_ge(job_done, 16 + 8 * (t - 1))
                    sp.dma_start(ring[:, t % 2], d["w_in"][0, :, c * HALF:(c + 1) * HALF].rearrange(
                        "(k p) n -> p k n", p=P)).then_inc(w_in[t], 16)
                for n in range(2):
                    sp.wait_ge(job_done, 16 + 8 * (n + 3))
                    sp.dma_start(ring[:, n], d["w_out"][0, :, n * HALF:(n + 1) * HALF].rearrange(
                        "(k p) n -> p k n", p=P)).then_inc(w_in[4 + n], 16)
                for b in range(TB):
                    sp.wait_ge(x1_ready, 2 * (b + 1))
                    sp.dma_start(rows.x1[b * P:(b + 1) * P, :], x[:, b, :]).then_inc(st[b], 16)
                for b in range(TB):
                    sp.wait_ge(h2_ready, b + 1)
                    sp.dma_start(rows.h2[b * P:(b + 1) * P, :], xn[:, b, :]).then_inc(st[TB + b], 16)
                for s in st:
                    sp.wait_ge(s, 16)

            @block.gpsimd
            def _(pool):
                pool.memset(ident[:, :], 0.0).then_inc(consts, 1)
                pool.memset(mask[:, :], 0.0).then_inc(consts, 1)
                pool.iota(inv_i[:, :], [[1, WMAX]], base=1, channel_multiplier=0).then_inc(consts, 1)
                pool.memset(hT[:, 0, :], 0.0).then_inc(zeroed, 1)
                pool.wait_ge(consts, 3)
                pool.affine_select(out=ident[:, :], in_=ident[:, :], compare_op=ALU.not_equal, fill=1.0,
                                   base=0, pattern=[[-1, P]], channel_multiplier=1).then_inc(consts, 1)
                pool.affine_select(out=mask[:, :], in_=mask[:, :], compare_op=ALU.is_ge, fill=MASKED,
                                   base=0, pattern=[[-1, P]], channel_multiplier=1).then_inc(consts, 1)
                pool.wait_ge(zeroed, 1)
                for i, dst in enumerate((rows.x1, rows.h2)):
                    for r in range(SLOTS // P):
                        z = 2 * i + r
                        pool.dma_start(dst[S + r * P:S + (r + 1) * P, :], hT[:, 0, :]).then_inc(zero_st[z], 16)
                for z in zero_st:
                    pool.wait_ge(z, 16)
                pool.sem_inc(zeroed, 1)

            @block.scalar
            def _(act):
                act.dma_start(lam_in[:, 0, :], d["lambda_q1"].partition_broadcast(P)).then_inc(lam_ld, 16)
                act.dma_start(lam_in[:, 1, :], d["lambda_q2"].partition_broadcast(P)).then_inc(lam_ld, 16)
                act.dma_start(lam_in[:, 2, :], d["lambda_k1"].partition_broadcast(P)).then_inc(lam_ld, 16)
                act.dma_start(lam_in[:, 3, :], d["lambda_k2"].partition_broadcast(P)).then_inc(lam_ld, 16)
                act.dma_start(wp[:, :, :], d["w_pool"][0].rearrange("g c n -> c g n")).then_inc(wp_in, 16)
                act.dma_start(rw[:, :, :], d["router_w"][0].rearrange("(k p) e -> p k e", p=P)).then_inc(rw_in, 16)
                act.dma_start(rb[:, :], d["router_b"].partition_broadcast(P)).then_inc(rb_in, 16)
                act.dma_start(g2[:, :], d["norm2_g"].partition_broadcast(P)).then_inc(g2_in, 16)
                for b in range(TB):
                    act.wait_ge(x_in[b], 16)
                    if b:
                        act.wait_ge(squares, b)
                    act.activation(junk, x[:, b, :], ACT.Square, accum_out=ss[:, b:b + 1]).then_inc(squares, 1)
                act.wait_ge(lam_s, 2)
                act.activation(lam[:, 2:4], lam[:, 0:2], ACT.Exp).then_inc(lam_exp, 1)

                def empty(n):
                    what, a, b, who = jobs[n]
                    if who != "act":
                        return
                    act.wait_ge(job_done, n + 1)
                    bank = ps[:, n % 8, :]
                    if what == "norm":
                        if n == 1:
                            act.wait_ge(vec_ready, 1)
                            act.wait_ge(zeroed, 2)
                        ins = act.activation(hT[:, b, a * HALF:(a + 1) * HALF], bank, ACT.Copy, scale=g_in[:, b:b + 1])
                    elif what in "qk":
                        ins = act.activation(qkT[:, "qk".index(what), a, b * HALF:(b + 1) * HALF], bank, ACT.Copy)
                    elif what == "u":
                        ins = act.activation(uT[:, a, b * HALF:(b + 1) * HALF], bank, ACT.Copy)
                    elif what == "v":
                        ins = act.activation(v[:, a, :], bank, ACT.Copy)
                    else:
                        ins = act.activation(h2T[:, b, a * HALF:(a + 1) * HALF], bank, ACT.Copy)
                    ins.then_inc(ev["act"], 1)

                for n in range(first_out):
                    empty(n)

                def exps(step):
                    u, m = divmod(step, 2)
                    i, h = units[u]
                    act.wait_ge(biased, step + 1)
                    if u >= 2:
                        act.wait_ge(combined, u - 1)
                    n = (i + 1) * P
                    s4 = step % 4
                    act.activation(probs[:, s4, 0:n], ps[:, 2 * m:2 * m + 2, :].rearrange("p a b -> p (a b)")[:, 0:n],
                                   ACT.Exp, bias=soft[:, s4, 0:1], scale=DQK ** -0.5,
                                   accum_out=soft[:, s4, 1:2]).then_inc(exped, 1)

                tb = 0
                exps(0)
                exps(1)
                for u, (i, h) in enumerate(units):
                    for t in range(0, i + 1, 4):
                        w = min(4, i + 1 - t)
                        tb += 1
                        act.wait_ge(turned, tb)
                        act.activation(combT[:, t:t + w, :], ps[:, 4 + (tb - 1) % 2, 0:w * P].rearrange(
                            "p (a b) -> p a b", b=P), ACT.Copy).then_inc(turn_ev, 1)
                    if u + 1 < len(units):
                        exps(2 * u + 2)
                        exps(2 * u + 3)
                    if h == 1 and i >= 1 or u + 1 == len(units):
                        for b in ([i - 1] if u + 1 < len(units) else [TB - 1]):
                            act.wait_ge(oT_done, b + 1)
                            act.activation(mixT[:, 0:HEADS, b * P:(b + 1) * P], ps[:, 6 + b % 2, :].rearrange(
                                "p (h t) -> p h t", h=HEADS), ACT.Copy, scale=g_sub).then_inc(mixed, 1)
                for b in range(TB):
                    act.wait_ge(x1_ready, 2 * (b + 1))
                    if b:
                        act.wait_ge(sq2, b)
                    act.activation(junk, x[:, b, :], ACT.Square, accum_out=ss[:, b:b + 1]).then_inc(sq2, 1)
                for n in range(first_out, len(jobs)):
                    empty(n)

            @block.vector
            def _(dve):
                o = Order(dve, order_s)
                dve.wait_ge(lam_ld, 64)
                dve.tensor_tensor(lam_in[:, 0:2, :], lam_in[:, 0:2, :], lam_in[:, 2:4, :], ALU.mult).then_inc(lam_s, 1)
                dve.wait_ge(lam_s, 1)
                dve.reduce_sum(lam[:, 0:2], lam_in[:, 0:2, :], axis=AX).then_inc(lam_s, 1)
                dve.wait_ge(vec_mm, 1)
                o.did(dve.tensor_copy(vec[:, :], ps[:, 7, 0:17]))
                o.need()
                dve.tensor_scalar(g_sub, g_sub, 1.0 - LAMBDA_INIT, None, ALU.mult).then_inc(vec_ready, 1)
                dve.wait_ge(consts, 5)
                o.did(dve.tensor_copy(inv[:, 4, :], inv_i[:, :]))
                o.need()
                o.did(dve.reciprocal(inv[:, 4, :], inv[:, 4, :]))
                o.need()
                for g in range(POOLS):
                    o.did(dve.tensor_scalar(inv[:, g, :], inv[:, 4, :], 1.0 / 2 ** (g + 1), None, ALU.max))
                for half in range(2):
                    dve.wait_ge(squares, 4 * (half + 1))
                    c = slice(4 * half, 4 * half + 4)
                    rsqrt_mean(dve, o, rstd[:, c], ss[:, c], tmp[:, :, c], D)
                    o.need()
                    for b in range(4 * half, 4 * half + 4):
                        dve.tensor_scalar(xn[:, b, :], x[:, b, :], rstd[:, b:b + 1], None, ALU.mult).then_inc(normed, 1)
                dve.wait_ge(lam_exp, 1)
                o.did(dve.tensor_tensor(lam[:, 4:5], lam[:, 3:4], lam[:, 2:3], ALU.subtract))
                o.need()
                o.did(dve.tensor_scalar(lam[:, 5:6], lam[:, 4:5], -LAMBDA_INIT, None, ALU.add))
                neg_lam = lam[:, 5:6]

                def empty(n):
                    what, a, b, who = jobs[n]
                    if who != "dve":
                        return
                    dve.wait_ge(job_done, n + 1)
                    bank = ps[:, n % 8, :]
                    if what == "norm":
                        if n == 0:
                            dve.wait_ge(vec_ready, 1)
                            dve.wait_ge(zeroed, 2)
                        ins = dve.tensor_scalar(hT[:, b, a * HALF:(a + 1) * HALF], bank, g_in[:, b:b + 1], None, ALU.mult)
                    elif what in "qk":
                        ins = dve.tensor_copy(qkT[:, "qk".index(what), a, b * HALF:(b + 1) * HALF], bank)
                    elif what == "u":
                        ins = dve.tensor_copy(uT[:, a, b * HALF:(b + 1) * HALF], bank)
                    elif what == "pool":
                        if a == 0 and b == 0:
                            dve.wait_ge(job_done, 48)
                        ins = dve.tensor_scalar(mixT[:, 4 + a, b * HALF:(b + 1) * HALF], bank, b_pool[:, a:a + 1],
                                                s_pool[:, a:a + 1], ALU.add, ALU.mult)
                    elif what == "out":
                        xs = x[:, a, b * HALF:(b + 1) * HALF]
                        dve.tensor_tensor(xs, bank, xs, ALU.add).then_inc(x1_ready, 1)
                        return
                    else:
                        ins = dve.tensor_copy(h2T[:, b, a * HALF:(a + 1) * HALF], bank)
                    ins.then_inc(ev["dve"], 1)

                for n in range(first_out - 8):
                    empty(n)
                dve.wait_ge(ev["act"], emptied(39)[1])
                dve.wait_ge(ev["dve"], emptied(38)[1])
                for g in range(POOLS):
                    src = uT[:, g, :]
                    if g:
                        dve.wait_ge(pooled, g)
                    for i in range(g + 1):
                        dst, w = (pool_a, pool_b)[i % 2], 2 ** i
                        o.need()
                        o.did(dve.tensor_tensor(dst[:, w:S], src[:, w:S], src[:, 0:S - w], ALU.add))
                        o.did(dve.tensor_copy(dst[:, 0:w], src[:, 0:w]))
                        src = dst
                    o.need()
                    o.did(dve.tensor_tensor(src[:, 0:WMAX], src[:, 0:WMAX], inv[:, g, :], ALU.mult))
                    o.need()
                    o.did(dve.tensor_tensor(uT[:, g, 0:WMAX], src[:, 0:WMAX], uT[:, g, 0:WMAX], ALU.subtract))
                    dve.scalar_tensor_tensor(uT[:, g, WMAX:S], src[:, WMAX:S], 1.0 / 2 ** (g + 1), uT[:, g, WMAX:S],
                                             ALU.mult, ALU.subtract).then_inc(pooled, 1)
                for n in range(first_out - 8, first_out):
                    empty(n)

                def bias(step):
                    u, m = divmod(step, 2)
                    i, h = units[u]
                    s4, n = step % 4, (i + 1) * P
                    sc = ps[:, 2 * m:2 * m + 2, :].rearrange("p a b -> p (a b)")
                    dve.wait_ge(scored, step + 1)
                    o.did(dve.tensor_tensor(sc[:, n - P:n], sc[:, n - P:n], mask[:, :], ALU.add))
                    o.need()
                    o.did(dve.reduce_max(soft[:, 4 + s4, 0:1], sc[:, 0:n], axis=AX))
                    o.need()
                    dve.tensor_scalar(soft[:, s4, 0:1], soft[:, 4 + s4, 0:1], -DQK ** -0.5, None, ALU.mult).then_inc(biased, 1)

                def combine(u):
                    i, h = units[u]
                    n, a, b = (i + 1) * P, (2 * u) % 4, (2 * u + 1) % 4
                    dve.wait_ge(exped, 2 * u + 2)
                    o.did(dve.reciprocal(r0[:, i % 2, h:h + 1], soft[:, a, 1:2]))
                    o.did(dve.reciprocal(soft[:, 4 + b, 1:2], soft[:, b, 1:2]))
                    o.need()
                    o.did(dve.scalar_tensor_tensor(soft[:, 4 + a, 1:2], soft[:, a, 1:2], soft[:, 4 + b, 1:2], neg_lam,
                                                   ALU.mult, ALU.mult))
                    o.need()
                    if u >= 2:
                        dve.wait_ge(turned, sum(-(-(units[x][0] + 1) // 4) for x in range(u - 1)))
                    dve.scalar_tensor_tensor(comb[:, u % 2, 0:n], probs[:, b, 0:n], soft[:, 4 + a, 1:2],
                                             probs[:, a, 0:n], ALU.mult, ALU.add).then_inc(combined, 1)

                def out_norm(i):
                    o4 = ot.rearrange("p (h t) -> p h t", h=HEADS)
                    sq = pool_a[:, 0:HALF].rearrange("p (h t) -> p h t", h=HEADS)
                    dve.wait_ge(o_done, i + 1)
                    if i:
                        dve.wait_ge(oT_done, i)
                    o.did(dve.tensor_tensor(o4, ps[:, 6 + i % 2, :].rearrange("p (h t) -> p h t", h=HEADS),
                                            bcast(r0[:, i % 2, :], P), ALU.mult))
                    o.need()
                    o.did(dve.tensor_tensor(sq, o4, o4, ALU.mult))
                    o.need()
                    o.did(dve.reduce_sum(ss[:, 0:HEADS], sq, axis=AX))
                    rsqrt_mean(dve, o, rstd[:, 0:HEADS], ss[:, 0:HEADS], tmp[:, :, 0:HEADS], DV)
                    o.need()
                    dve.tensor_tensor(o4, o4, bcast(rstd[:, 0:HEADS], P), ALU.mult).then_inc(o_norm, 1)

                bias(0)
                bias(1)
                for u, (i, h) in enumerate(units):
                    combine(u)
                    if u + 1 < len(units):
                        bias(2 * u + 2)
                        bias(2 * u + 3)
                    if h == 0 and i >= 1:
                        out_norm(i - 1)
                out_norm(TB - 1)
                for n in range(first_out, first_out + 16):
                    empty(n)
                dve.wait_ge(g2_in, 16)
                for half in range(2):
                    dve.wait_ge(sq2, 4 * (half + 1))
                    c = slice(4 * half, 4 * half + 4)
                    rsqrt_mean(dve, o, rstd[:, c], ss[:, c], tmp[:, :, c], D)
                    o.need()
                    for b in range(4 * half, 4 * half + 4):
                        dve.scalar_tensor_tensor(xn[:, b, :], x[:, b, :], rstd[:, b:b + 1], g2[:, :], ALU.mult,
                                                 ALU.mult).then_inc(h2_ready, 1)
                for n in range(first_out + 16, len(jobs)):
                    empty(n)
                dve.wait_ge(router_mm, 1)
                dve.wait_ge(rb_in, 16)
                dve.tensor_tensor(keep.logits[:, :, :], ps[:, 0, 0:TB * E].rearrange("p (b e) -> p b e", e=E),
                                  repeat(rb[:, :], TB), ALU.add).then_inc(router_ev, 1)
                dve.wait_ge(router_ev, 1)

            @block.tensor
            def _(pe):
                pe.wait_ge(consts, 5)
                pe.wait_ge(vec_in, 64)
                pe.transpose(ps[:, 7, 0:17], vec_rows[:, :], ident[0:17, 0:17]).then_inc(vec_mm, 1)
                pe.wait_ge(vec_ready, 1)

                def bank_for(n):
                    if n >= 8 and n != first_out:
                        if jobs[n - 8][0] == "out":
                            pe.wait_ge(x1_ready, n - 8 - first_out + 1)
                        elif n - 8 < first_out <= n:
                            pass
                        else:
                            who, count = emptied_no_out(n - 8)
                            pe.wait_ge(ev[who], count)
                    return ps[:, n % 8, :]

                def emptied_no_out(n):
                    who = jobs[n][3]
                    return who, sum(j[3] == who and j[0] != "out" for j in jobs[:n + 1])

                for n in range(first_out):
                    what, a, b, _ = jobs[n]
                    if what in tile_of and (a, b) == (0, 0):
                        pe.wait_ge(w_in[tile_of[what]], 16)
                        if what == "q":
                            pe.wait_ge(ev["act"], 8)
                            pe.wait_ge(ev["dve"], 8)
                    bank = bank_for(n)
                    if what == "norm":
                        for t in range(4):
                            pe.wait_ge(normed, 4 * a + t + 1)
                            ins = pe.transpose(bank[:, t * P:(t + 1) * P], xn[:, 4 * a + t, b * P:(b + 1) * P], ident[:, :])
                    elif what == "v":
                        for k in range(KC):
                            ins = pe.matmul(bank, hT[:, k, a * P:(a + 1) * P], ring[:, 1, k, :], start=k == 0, stop=k == KC - 1)
                    elif what == "pool":
                        pe.wait_ge(wp_in, 16)
                        pe.wait_ge(pooled, a + 1)
                        ins = pe.matmul(bank, wp[:, a, :], uT[:, a, b * HALF:(b + 1) * HALF], start=True, stop=True)
                    else:
                        for k in range(KC):
                            ins = pe.matmul(bank, ring[:, tile_of[what] % 2, k, a * P:(a + 1) * P],
                                            hT[:, k, b * HALF:(b + 1) * HALF], start=k == 0, stop=k == KC - 1)
                    ins.then_inc(job_done, 1)
                pe.wait_ge(ev["dve"], emptied_no_out(first_out - 1)[1])
                pe.wait_ge(ev["act"], sum(j[3] == "act" for j in jobs[:first_out]))

                def scores(step):
                    u, m = divmod(step, 2)
                    i, h = units[u]
                    if step >= 2:
                        pe.wait_ge(exped, step - 1)
                    part = slice(m * DQK, (m + 1) * DQK)
                    for c in range(0, (i + 1) * P, HALF):
                        w = min(HALF, (i + 1) * P - c)
                        ins = pe.matmul(ps[:, 2 * m + c // HALF, 0:w], qkT[part, 0, h, i * P:(i + 1) * P],
                                        qkT[part, 1, h, c:c + w], start=True, stop=True)
                    ins.then_inc(scored, 1)

                def turn_out(i):
                    pe.wait_ge(o_norm, i + 1)
                    for h in range(HEADS):
                        ins = pe.transpose(ps[:, 6 + i % 2, h * P:(h + 1) * P], ot[:, h * P:(h + 1) * P], ident[:, :])
                    ins.then_inc(oT_done, 1)

                tb = 0
                scores(0)
                scores(1)
                for u, (i, h) in enumerate(units):
                    if u + 1 < len(units):
                        scores(2 * u + 2)
                    pe.wait_ge(combined, u + 1)
                    for t in range(0, i + 1, 4):
                        if tb >= 2:
                            pe.wait_ge(turn_ev, tb - 1)
                        for k in range(t, min(t + 4, i + 1)):
                            ins = pe.transpose(ps[:, 4 + tb % 2, (k - t) * P:(k - t + 1) * P],
                                               comb[:, u % 2, k * P:(k + 1) * P], ident[:, :])
                        ins.then_inc(turned, 1)
                        tb += 1
                    if h == 1 and i >= 1:
                        turn_out(i - 1)
                    if u + 1 < len(units):
                        scores(2 * u + 3)
                    pe.wait_ge(turn_ev, tb)
                    if h == 0 and i >= 2:
                        pe.wait_ge(mixed, i - 1)
                    for k in range(i + 1):
                        ins = pe.matmul(ps[:, 6 + i % 2, h * P:(h + 1) * P], combT[:, k, :], v[:, k, h * P:(h + 1) * P],
                                        start=k == 0, stop=k == i)
                    if h == HEADS - 1:
                        ins.then_inc(o_done, 1)
                turn_out(TB - 1)
                pe.wait_ge(mixed, TB)
                pe.wait_ge(w_in[4], 16)
                pe.wait_ge(w_in[5], 16)
                for n in range(first_out, len(jobs)):
                    what, a, b, _ = jobs[n]
                    bank = bank_for(n)
                    if what == "out":
                        for k in range(KC):
                            ins = pe.matmul(bank, mixT[:, k, a * P:(a + 1) * P], ring[:, b, k, :], start=k == 0, stop=k == KC - 1)
                    else:
                        pe.wait_ge(h2_ready, 4 * a + 4)
                        for t in range(4):
                            ins = pe.transpose(bank[:, t * P:(t + 1) * P], xn[:, 4 * a + t, b * P:(b + 1) * P], ident[:, :])
                    ins.then_inc(job_done, 1)
                pe.wait_ge(ev["dve"], emptied_no_out(len(jobs) - 2)[1])
                pe.wait_ge(ev["act"], emptied_no_out(len(jobs) - 1)[1])
                pe.wait_ge(rw_in, 16)
                for b in range(TB):
                    for k in range(KC):
                        ins = pe.matmul(ps[:, 0, b * E:(b + 1) * E], h2T[:, k, b * P:(b + 1) * P], rw[:, k, :],
                                        start=k == 0, stop=k == KC - 1)
                ins.then_inc(router_mm, 1)


def routing(nc, d, keep, rows, r):
    with ExitStack() as ctx:
        sb = lambda name, shape, dt=F32: ctx.enter_context(nc.sbuf_tensor(name, shape, dt))
        sem = lambda name: ctx.enter_context(nc.semaphore(name))
        ps = ctx.enter_context(nc.psum_tensor("ps_routing", [P, 4, HALF], F32))
        tri, ones = sb("tri", [P, P]), sb("ones", [P, P])
        iota_i, iota_e = sb("iota_i", [P, SLOTS], I32), sb("iota_e", [P, E])
        small_i, small = sb("small_i", [P, 4 + TB], I32), sb("small", [P, 4])
        bias_rows = sb("bias_rows", [E, 3, D])
        top, where = sb("top", [P, TB, 8]), sb("where", [P, TB, 8], U32)
        where_f, gates = sb("where_f", [P, TB, 8]), sb("gates", [P, TB, TOPK])
        total = sb("total", [P, TB])
        hit, member = sb("hit", [P, TB, E]), sb("member", [P, TB, E])
        off = sb("off", [P, TB + 1, E])
        blocks, ends, starts = sb("blocks", [P, E]), sb("ends", [P, E]), sb("starts", [P, E])
        ones_e, hit_e, prod = sb("ones_e", [P, E]), sb("hit_e", [P, E]), sb("prod", [P, E])
        item = sb("item", [P, 8])
        meta_i = sb("meta_i", [P, 4], I32)
        made, biases_in, topped, exped = sem("made"), sem("biases_in"), sem("topped"), sem("exped_g")
        order_s, member_ready, rank_mm, bias_mm, meta_ready = (sem(n) for n in ("order_r", "member_ready", "rank_mm", "bias_mm", "meta_ready"))
        meta_st, meta_ld = sem("meta_st"), sem("meta_ld")

        with nc.Block() as block:

            @block.gpsimd
            def _(pool):
                pool.memset(tri[:, :], 1.0).then_inc(made, 1)
                pool.memset(ones[:, :], 1.0).then_inc(made, 1)
                pool.memset(ones_e[:, :], 1.0).then_inc(made, 1)
                pool.iota(iota_i[:, :], [[1, SLOTS]], base=0, channel_multiplier=0).then_inc(made, 1)
                pool.iota(small_i[:, 0:1], [[0, 1]], base=0, channel_multiplier=1).then_inc(made, 1)
                pool.iota(small_i[:, 1:3], [[P, 2]], base=S + 1, channel_multiplier=1).then_inc(made, 1)
                pool.iota(small_i[:, 4:4 + TB], [[P, TB]], base=1, channel_multiplier=1).then_inc(made, 1)
                pool.memset(small_i[:, 3:4], 0).then_inc(made, 1)
                pool.memset(r.meta[:, :, :], 0).then_inc(made, 1)
                pool.wait_ge(made, 9)
                pool.affine_select(out=tri[:, :], in_=tri[:, :], compare_op=ALU.is_ge, fill=0.0, base=-1,
                                   pattern=[[1, P]], channel_multiplier=-1).then_inc(made, 1)

            @block.sync
            def _(sp):
                for i, b in enumerate((d["b_gate"], d["b_up"], d["b_down"])):
                    sp.dma_start(bias_rows[:, i, :], b[0]).then_inc(biases_in, 16)
                sp.wait_ge(meta_ready, 1)
                with nc.allow_non_contiguous_dma("a column becomes a row"):
                    sp.dma_start(rows.meta.rearrange("a p -> p a"), meta_i[:, 0:3]).then_inc(meta_st, 16)
                sp.wait_ge(meta_st, 16)
                sp.dma_start(r.meta[0:1, :, 1:1 + P], rows.meta.rearrange("(o a) p -> o a p", o=1)).then_inc(meta_ld, 16)
                sp.wait_ge(meta_ld, 16)

            @block.scalar
            def _(act):
                act.wait_ge(topped, 1)
                act.activation(gates[:, :, :], gates[:, :, :], ACT.Exp).then_inc(exped, 1)

            @block.tensor
            def _(pe):
                pe.wait_ge(biases_in, 48)
                for i in range(3):
                    for m in range(KC):
                        ins = pe.transpose(ps[:, 2 + i // 2, ((i % 2) * KC + m) * E:((i % 2) * KC + m + 1) * E],
                                           bias_rows[:, i, m * P:(m + 1) * P], keep.ident[0:E, 0:E])
                ins.then_inc(bias_mm, 1)
                pe.wait_ge(made, 10)
                pe.wait_ge(member_ready, 1)
                flat = member[:, :, :].rearrange("p b e -> p (b e)")
                pe.matmul(ps[:, 0, 0:TB * E], tri[:, :], flat, start=True, stop=True)
                pe.matmul(ps[:, 1, 0:TB * E], ones[:, :], flat, start=True, stop=True).then_inc(rank_mm, 1)

            @block.vector
            def _(dve):
                o = Order(dve, order_s)
                dve.wait_ge(made, 10)
                o.did(dve.tensor_copy(r.iota[:, :], iota_i[:, :]))
                o.did(dve.tensor_copy(small[:, :], small_i[:, 0:4]))
                o.did(dve.tensor_copy(r.pad[:, :], small_i[:, 1:3]))
                o.did(dve.tensor_copy(r.tok_gate[:, :, 0:1], small_i[:, 4:4 + TB].unsqueeze(2)))
                o.did(dve.tensor_copy(iota_e[:, :], iota_i[:, 0:E]))
                for b in range(TB):
                    o.did(dve.max(top[:, b, :], keep.logits[:, b, :]))
                o.need()
                for b in range(TB):
                    o.did(dve.max_index(where[:, b, :], top[:, b, :], keep.logits[:, b, :]))
                dve.tensor_tensor(gates[:, :, :], top[:, :, 0:TOPK], top[:, :, 0:1].broadcast_to([P, TB, TOPK]),
                                  ALU.subtract).then_inc(topped, 1)
                o.need()
                o.did(dve.tensor_copy(where_f[:, :, :], where[:, :, :]))
                dve.wait_ge(exped, 1)
                o.did(dve.reduce_sum(total[:, :], gates[:, :, :], axis=AX))
                o.need()
                o.did(dve.reciprocal(total[:, :], total[:, :]))
                o.need()
                o.did(dve.tensor_tensor(gates[:, :, :], gates[:, :, :], bcast(total[:, :], TOPK), ALU.mult))
                for k in range(TOPK):
                    o.need()
                    o.did(dve.tensor_tensor(hit[:, :, :], repeat(iota_e[:, :], TB),
                                            where_f[:, :, k:k + 1].broadcast_to([P, TB, E]), ALU.is_equal))
                    o.need()
                    gate_k = gates[:, :, k:k + 1].broadcast_to([P, TB, E])
                    if k == 0:
                        o.did(dve.tensor_copy(member[:, :, :], hit[:, :, :]))
                        o.did(dve.tensor_tensor(r.gate[:, :, :], hit[:, :, :], gate_k, ALU.mult))
                    else:
                        o.did(dve.tensor_tensor(member[:, :, :], member[:, :, :], hit[:, :, :], ALU.add))
                        o.need()
                        o.did(dve.tensor_tensor(hit[:, :, :], hit[:, :, :], gate_k, ALU.mult))
                        o.need()
                        o.did(dve.tensor_tensor(r.gate[:, :, :], r.gate[:, :, :], hit[:, :, :], ALU.add))
                o.need()
                dve.sem_inc(member_ready, 1)
                o.did(dve.memset(off[:, 0, :], 0.0))
                dve.wait_ge(rank_mm, 1)
                for b in range(TB):
                    o.need()
                    o.did(dve.tensor_tensor(off[:, b + 1, :], off[:, b, :], ps[:, 1, b * E:(b + 1) * E], ALU.add))
                counts = off[:, TB, :]
                o.need()
                o.did(dve.tensor_tensor(r.slot[:, :, :], ps[:, 0, 0:TB * E].rearrange("p (b e) -> p b e", e=E),
                                        off[:, 0:TB, :], ALU.add))
                o.did(dve.tensor_scalar(blocks[:, :], counts, 0.0, None, ALU.is_gt))
                for m in range(1, S // SLOTS):
                    o.need()
                    o.did(dve.scalar_tensor_tensor(blocks[:, :], counts, float(m * SLOTS), blocks[:, :], ALU.is_gt, ALU.add))
                o.need()
                o.did(dve.tensor_tensor_scan(ends[:, :], ones_e[:, :], blocks[:, :], 0.0, ALU.mult, ALU.add))
                o.need()
                o.did(dve.tensor_tensor(starts[:, :], ends[:, :], blocks[:, :], ALU.subtract))
                o.need()
                o.did(dve.tensor_scalar(prod[:, :], starts[:, :], float(SLOTS), 1.0, ALU.mult, ALU.add))
                o.need()
                o.did(dve.tensor_tensor(r.slot[:, :, :], r.slot[:, :, :], repeat(prod[:, :], TB), ALU.add))
                o.need()
                o.did(dve.tensor_tensor(r.slot[:, :, :], r.slot[:, :, :], member[:, :, :], ALU.mult))
                o.need()
                o.did(dve.tensor_scalar(r.slot[:, :, :], r.slot[:, :, :], -1.0, None, ALU.add))
                o.did(dve.tensor_scalar(hit_e[:, :], ends[:, :], small[:, 0:1], None, ALU.is_le))
                o.need()
                o.did(dve.reduce_sum(item[:, 0:1], hit_e[:, :], axis=AX))
                o.need()
                o.did(dve.tensor_scalar(hit_e[:, :], iota_e[:, :], item[:, 0:1], None, ALU.is_equal))
                o.need()
                o.did(dve.tensor_tensor(prod[:, :], hit_e[:, :], counts, ALU.mult))
                o.need()
                o.did(dve.reduce_sum(item[:, 1:2], prod[:, :], axis=AX))
                o.need()
                o.did(dve.tensor_tensor(prod[:, :], hit_e[:, :], starts[:, :], ALU.mult))
                o.need()
                o.did(dve.reduce_sum(item[:, 2:3], prod[:, :], axis=AX))
                o.need()
                o.did(dve.tensor_tensor(item[:, 3:4], item[:, 2:3], small[:, 0:1], ALU.subtract))
                o.need()
                o.did(dve.scalar_tensor_tensor(item[:, 4:5], item[:, 3:4], float(SLOTS), item[:, 1:2], ALU.mult, ALU.add))
                o.need()
                o.did(dve.tensor_scalar(item[:, 5:6], item[:, 4:5], 0.0, None, ALU.is_gt))
                for n in LEVELS[:-1]:
                    o.need()
                    o.did(dve.scalar_tensor_tensor(item[:, 5:6], item[:, 4:5], float(n), item[:, 5:6], ALU.is_gt, ALU.add))
                o.need()
                o.did(dve.tensor_scalar(item[:, 6:7], item[:, 0:1], float(E - 1), None, ALU.min))
                o.need()
                o.did(dve.tensor_copy(meta_i[:, 0:1], item[:, 5:6]))
                o.did(dve.tensor_copy(meta_i[:, 1:2], item[:, 6:7]))
                o.did(dve.tensor_copy(meta_i[:, 2:3], ends[:, E - 1:E]))
                o.need()
                dve.sem_inc(meta_ready, 1)
                dve.wait_ge(bias_mm, 1)
                o.did(dve.tensor_copy(r.bias[:, 0:2].rearrange("p i m e -> p (i m e)"), ps[:, 2, :]))
                o.did(dve.tensor_copy(r.bias[:, 2].rearrange("p m e -> p (m e)"), ps[:, 3, 0:KC * E]))
                o.need()


def experts(nc, d, keep, rows, r):
    with ExitStack() as ctx:
        sb = lambda name, shape, dt=F32: ctx.enter_context(nc.sbuf_tensor(name, shape, dt))
        sem = lambda name: ctx.enter_context(nc.semaphore(name))
        ps = ctx.enter_context(nc.psum_tensor("ps_experts", [P, 8, HALF], F32))
        w = [sb(f"w_tile{g}", [P, KC, HALF]) for g in range(GROUPS)]
        onehot = sb("onehot", [P, TB, SLOTS])
        slot_col = sb("slot_col", [P, TB])
        tab_next, tab_now, tab_last = (sb(n, [P, 4], I32) for n in ("tab_next", "tab_now", "tab_last"))
        idx_f = sb("idx_f", [P, 2])
        bias = sb("bias_now", [P, 3, KC])
        xg = sb("xg", [P, 2, D])
        xT = sb("xT", [P, KC, SLOTS])
        gt, ut, sg = (sb(n, [P, 4, SLOTS]) for n in ("gt", "ut", "sg"))
        aT = sb("aT", [P, KC, SLOTS])
        yT = sb("yT", [P, KC, SLOTS])
        y = sb("y", [P, 2, D])
        pair = [ps[:, 2 * i:2 * i + 2, :].rearrange("p a (b n) -> p (a b) n", n=SLOTS) for i in range(3)]
        side = 6

        w_ready = [sem(f"w_ready{g}") for g in range(GROUPS)]
        onehot_ready, idx_mm, idx_ready = sem("onehot_ready"), sem("idx_mm"), sem("idx_ready")
        gathered, scattered, rows_out = sem("gathered"), sem("scattered"), sem("rows_out")
        xT_mm, xT_ready, group_done, pair_free = sem("xT_mm"), sem("xT_ready"), sem("group_done"), sem("pair_free")
        g_ready, sg_ready, a_ready = sem("g_ready"), sem("sg_ready"), sem("a_ready")
        back_mm, y_ready, tab_ready, order_s, passed = sem("back_mm"), sem("y_ready"), sem("tab_ready"), sem("order_e"), sem("passed")

        def level(eng, n):
            return eng.value_load(r.meta[0:1, 0, bass.ds(n, 1)] if not isinstance(n, int) else r.meta[0:1, 0, n:n + 1],
                                  min_val=0, max_val=len(LEVELS))

        def expert(eng, n):
            return eng.value_load(r.meta[0:1, 1, bass.ds(n, 1)] if not isinstance(n, int) else r.meta[0:1, 1, n:n + 1],
                                  min_val=0, max_val=E - 1)

        def at_level(eng, lv, body):
            for i, n in enumerate(LEVELS):
                with eng.If(lv == i + 1):
                    body(n)

        def rounds(eng, body):
            last = eng.value_load(r.meta[0:1, 2, 1:2], min_val=1, max_val=ITEMS)
            with eng.Fori(0, ITEMS + 1) as j:
                with eng.If(j <= last):
                    body(j)
                    eng.sem_inc(passed, 1)
            return last

        def hold(eng, s, value):
            eng.wait_ge(s, value)
            eng.sem_inc(passed, 1)

        sources = [(d["w_gate"], 0), (d["w_up"], 0), (d["w_gate"], 1), (d["w_up"], 1), (d["w_down"], 0), (d["w_down"], 1)]

        with nc.Block() as block:

            @block.sync
            def _(sp):
                def load(e, g):
                    src, c = sources[g]
                    at = src[0, bass.ds(e, 1), :, c * HALF:(c + 1) * HALF].rearrange("o (k p) n -> p (o k) n", p=P)
                    sp.dma_start(w[g][:, :, :], at).then_inc(w_ready[g], 16)

                e0 = expert(sp, 1)
                for g in range(GROUPS):
                    load(e0, g)

                def body(j):
                    lv, e = level(sp, j + 2), expert(sp, j + 2)
                    with sp.If(lv > 0):
                        for g in range(GROUPS):
                            sp.wait_ge(group_done, j * GROUPS + g + 1)
                            load(e, g)
                rounds(sp, body)

            @block.gpsimd
            def _(pool):
                def gather(j, n):
                    hold(pool, idx_ready, j + 2)
                    if not isinstance(j, int):
                        hold(pool, xT_mm, j * 4 + 4)
                    for h in range(2):
                        m = min(P, n - h * P)
                        if m > 0:
                            pool.indirect_dma_start(out=xg[0:m, h, :], out_offset=None, in_=rows.h2[:, :],
                                                    in_offset=bass.IndirectOffsetOnAxis(ap=tab_next[0:m, h:h + 1].bitcast(U32), axis=0)
                                                    ).then_inc(gathered, 16 if n > P else 32)

                def scatter(j, n):
                    hold(pool, tab_ready, j + 1)
                    for h in range(2):
                        m = min(P, n - h * P)
                        if m > 0:
                            hold(pool, y_ready, j * 2 + h + 1)
                            pool.indirect_dma_start(out=rows.x1[:, :],
                                                    out_offset=bass.IndirectOffsetOnAxis(ap=tab_last[0:m, h:h + 1].bitcast(U32), axis=0),
                                                    in_=y[0:m, h, :], in_offset=None, compute_op=ALU.add
                                                    ).then_inc(scattered, 16 if n > P else 32)

                pool.sem_inc(rows_out, 1)
                at_level(pool, level(pool, 1), lambda n: gather(-1, n))

                def body(j):
                    last_lv, next_lv = level(pool, j), level(pool, j + 2)
                    at_level(pool, last_lv, lambda n: scatter(j, n))
                    at_level(pool, next_lv, lambda n: gather(j, n))
                    with pool.If(last_lv > 0):
                        hold(pool, scattered, j * 32)
                    pool.sem_inc(rows_out, 1)
                rounds(pool, body)

            @block.scalar
            def _(act):
                act.sem_inc(y_ready, 2)

                def turn_in(j, n):
                    for q in range(4):
                        act.wait_ge(xT_mm, (j + 1) * 4 + q + 1)
                        act.activation(xT[:, 2 * q:2 * q + 2, 0:n], ps[:, side + q % 2, :].rearrange(
                            "p (a n) -> p a n", a=2)[:, :, 0:n], ACT.Copy).then_inc(xT_ready, 1)

                def gate(j, n, c):
                    act.wait_ge(g_ready, j * 2 + c + 1)
                    act.activation(sg[:, :, 0:n], gt[:, :, 0:n], ACT.Sigmoid, scale=ALPHA).then_inc(sg_ready, 1)

                def back(j, n):
                    act.wait_ge(tab_ready, j + 1)
                    for h in range(2):
                        m = min(P, n - h * P)
                        if m <= 0:
                            continue
                        act.wait_ge(back_mm, j * 2 + h + 1)
                        act.wait_ge(rows_out, j + 1)
                        act.activation(y[0:m, h, :].rearrange("p (a n) -> p a n", a=2), ps[0:m, side:side + 2, :], ACT.Copy,
                                       scale=tab_last[0:m, 2 + h:3 + h].bitcast(F32)).then_inc(y_ready, 1 if n > P else 2)

                at_level(act, level(act, 1), lambda n: turn_in(-1, n))

                def body(j):
                    last_lv, lv, next_lv = level(act, j), level(act, j + 1), level(act, j + 2)
                    at_level(act, lv, lambda n: gate(j, n, 0))
                    at_level(act, last_lv, lambda n: back(j, n))
                    at_level(act, lv, lambda n: gate(j, n, 1))
                    at_level(act, next_lv, lambda n: turn_in(j, n))
                rounds(act, body)

            @block.vector
            def _(dve):
                dve.sem_inc(pair_free, 3)
                STEPS = 21
                o = Order(dve, order_s)

                def match(j):
                    e = expert(dve, j + 2)
                    o.did(dve.tensor_copy(slot_col[:, :], r.slot[:, :, bass.ds(e, 1)].rearrange("p b o -> p (b o)")))
                    o.did(dve.tensor_copy(r.tok_gate[:, :, 1:2], r.gate[:, :, bass.ds(e, 1)]))
                    if not isinstance(j, int):
                        o.did(dve.tensor_scalar(r.iota[:, :], r.iota[:, :], float(SLOTS), None, ALU.add))
                    else:
                        o.did(dve.tensor_scalar(r.iota[:, :], r.iota[:, :], 0.0, None, ALU.add))
                    o.need()
                    for b in range(TB):
                        o.did(dve.tensor_scalar(onehot[:, b, :], r.iota[:, :], slot_col[:, b:b + 1], None, ALU.is_equal))
                    o.need()
                    dve.sem_inc(onehot_ready, 1)

                def table(j):
                    dve.wait_ge(idx_mm, j + 2)
                    tg = ps[:, side, 0:4].rearrange("p (h c) -> p h c", c=2)
                    o.did(dve.tensor_scalar(idx_f[:, :], tg[:, :, 0], 0.0, None, ALU.is_equal))
                    o.did(dve.tensor_copy(tab_next[:, 2:4].bitcast(F32), tg[:, :, 1]))
                    o.need()
                    o.did(dve.tensor_tensor(idx_f[:, :], idx_f[:, :], r.pad[:, :], ALU.mult))
                    o.need()
                    dve.scalar_tensor_tensor(tab_next[:, 0:2], idx_f[:, :], -1.0, tg[:, :, 0], ALU.add, ALU.add).then_inc(idx_ready, 1)
                    hold(dve, idx_ready, j + 2)

                def gate_in(j, n, c):
                    dve.wait_ge(group_done, j * GROUPS + 2 * c + 1)
                    dve.tensor_tensor(gt[:, :, 0:n], pair[(2 * c) % 3][:, :, 0:n], bcast(bias[:, 0, 4 * c:4 * c + 4], n),
                                      ALU.add).then_inc(pair_free, 1)
                    dve.wait_ge(pair_free, j * GROUPS + 2 * c + 4)
                    dve.tensor_scalar(gt[:, :, 0:n], gt[:, :, 0:n], LIMIT, None, ALU.min).then_inc(g_ready, 1)

                def up_in(j, n, c):
                    dve.wait_ge(group_done, j * GROUPS + 2 * c + 2)
                    dve.tensor_tensor(ut[:, :, 0:n], pair[(2 * c + 1) % 3][:, :, 0:n], bcast(bias[:, 1, 4 * c:4 * c + 4], n),
                                      ALU.add).then_inc(pair_free, 1)
                    dve.wait_ge(pair_free, j * GROUPS + 2 * c + 5)
                    o.did(dve.tensor_scalar(ut[:, :, 0:n], ut[:, :, 0:n], LIMIT, -LIMIT, ALU.min, ALU.max))
                    dve.wait_ge(sg_ready, j * 2 + c + 1)
                    o.did(dve.tensor_tensor(sg[:, :, 0:n], gt[:, :, 0:n], sg[:, :, 0:n], ALU.mult))
                    o.need()
                    dve.scalar_tensor_tensor(aT[:, 4 * c:4 * c + 4, 0:n], ut[:, :, 0:n], 1.0, sg[:, :, 0:n], ALU.add,
                                             ALU.mult).then_inc(a_ready, 1)

                def down_in(j, n, c):
                    dve.wait_ge(group_done, j * GROUPS + c + 5)
                    dve.tensor_tensor(yT[:, 4 * c:4 * c + 4, 0:n], pair[1 + c][:, :, 0:n], bcast(bias[:, 2, 4 * c:4 * c + 4], n),
                                      ALU.add).then_inc(pair_free, 1)

                o.did(dve.memset(tab_now[:, :], 0))
                match(-1)
                table(-1)
                first_steps = o.n

                def body(j):
                    last_lv, lv, next_lv = level(dve, j), level(dve, j + 1), level(dve, j + 2)
                    e = expert(dve, j + 1)
                    base = first_steps

                    def restart(at):
                        o.base, o.n = j * STEPS + base, at

                    restart(0)
                    dve.wait_ge(rows_out, j + 1)
                    o.did(dve.tensor_copy(tab_last[:, :], tab_now[:, :]))
                    o.need()
                    o.did(dve.tensor_copy(tab_now[:, :], tab_next[:, :]))
                    o.did(dve.tensor_copy(bias[:, :, :].rearrange("p i m -> p (i m)"),
                                          r.bias[:, :, :, bass.ds(e, 1)].rearrange("p i m o -> p (i m o)")))
                    o.need()
                    dve.sem_inc(tab_ready, 1)
                    with dve.If(next_lv > 0):
                        match(j)
                    with dve.Else():
                        dve.sem_inc(order_s, 11)
                    after_match = 3 + 11

                    def first(n):
                        restart(after_match)
                        gate_in(j, n, 0)
                        up_in(j, n, 0)
                        gate_in(j, n, 1)
                    at_level(dve, lv, first)
                    with dve.If(next_lv > 0):
                        restart(after_match + 2)
                        table(j)
                    with dve.Else():
                        dve.sem_inc(order_s, 3)

                    def second(n):
                        restart(after_match + 5)
                        up_in(j, n, 1)
                        down_in(j, n, 0)
                        down_in(j, n, 1)
                    at_level(dve, lv, second)
                    assert o.n == after_match + 7, o.n
                rounds(dve, body)

            @block.tensor
            def _(pe):
                def product(j, g, n, rhs, first_half=None):
                    pe.wait_ge(w_ready[g], j * 16 + 16)
                    pe.wait_ge(pair_free, j * GROUPS + g + 1)
                    for m in range(4):
                        for k in range(KC):
                            if first_half is not None and m == 0 and k % 4 == 0:
                                pe.wait_ge(a_ready, j * 2 + k // 4 + 1)
                            ins = pe.matmul(pair[g % 3][:, m, 0:n], w[g][:, k, m * P:(m + 1) * P], rhs[:, k, 0:n],
                                            start=k == 0, stop=k == KC - 1)
                    ins.then_inc(group_done, 1)

                def index(j):
                    pe.wait_ge(onehot_ready, j + 2)
                    if not isinstance(j, int):
                        pe.wait_ge(y_ready, j * 2 + 2)
                        pe.wait_ge(xT_ready, j * 4 + 4)
                    for h in range(2):
                        for b in range(TB):
                            ins = pe.matmul(ps[:, side, 2 * h:2 * h + 2], onehot[:, b, h * P:(h + 1) * P], r.tok_gate[:, b, :],
                                            start=b == 0, stop=b == TB - 1)
                    ins.then_inc(idx_mm, 1)

                def turn_in(j, n):
                    pe.wait_ge(gathered, (j + 2) * 32)
                    pe.wait_ge(idx_ready, j + 2)
                    for q in range(4):
                        if q >= 2:
                            pe.wait_ge(xT_ready, (j + 1) * 4 + q - 1)
                        for a in range(2):
                            for h in range(2):
                                m = min(P, n - h * P)
                                if m > 0:
                                    k = 2 * q + a
                                    ins = pe.transpose(ps[:, side + q % 2, a * SLOTS + h * P:a * SLOTS + h * P + m],
                                                       xg[0:m, h, k * P:(k + 1) * P], keep.ident[0:m, 0:m])
                        ins.then_inc(xT_mm, 1)

                def back(j, n):
                    hold(pe, pair_free, j * GROUPS + 3)
                    for h in range(2):
                        m = min(P, n - h * P)
                        if m <= 0:
                            continue
                        if h:
                            hold(pe, y_ready, j * 2 + 1)
                        for k in range(KC):
                            ins = pe.transpose(ps[0:m, side + k // 4, (k % 4) * P:(k % 4 + 1) * P], yT[:, k, h * P:h * P + m],
                                               keep.ident[:, :])
                        ins.then_inc(back_mm, 1 if n > P else 2)

                pe.sem_inc(back_mm, 2)
                index(-1)
                at_level(pe, level(pe, 1), lambda n: turn_in(-1, n))

                def body(j):
                    last_lv, lv, next_lv = level(pe, j), level(pe, j + 1), level(pe, j + 2)

                    def first(n):
                        pe.wait_ge(xT_ready, j * 4 + 4)
                        product(j, 0, n, xT)
                        product(j, 1, n, xT)
                    at_level(pe, lv, first)
                    at_level(pe, last_lv, lambda n: back(j, n))
                    at_level(pe, lv, lambda n: product(j, 2, n, xT))
                    with pe.If(next_lv > 0):
                        index(j)
                    at_level(pe, lv, lambda n: product(j, 3, n, xT))
                    at_level(pe, next_lv, lambda n: turn_in(j, n))

                    def down(n):
                        product(j, 4, n, aT, first_half=True)
                        product(j, 5, n, aT)
                    at_level(pe, lv, down)
                rounds(pe, body)


def final(nc, d, keep, rows, out):
    with ExitStack() as ctx:
        sb = lambda name, shape, dt=F32: ctx.enter_context(nc.sbuf_tensor(name, shape, dt))
        sem = lambda name: ctx.enter_context(nc.semaphore(name))
        x2, y2, g = sb("x2", [P, TB, D]), sb("y2", [P, TB, D]), sb("g_final", [P, D])
        junk, ss, rstd, tmp = sb("junk_f", [P, D]), sb("ss_f", [P, TB]), sb("rstd_f", [P, TB]), sb("tmp_f", [P, 3, TB])
        x_in, st = [sem(f"xf_in{b}") for b in range(TB)], [sem(f"out_st{b}") for b in range(TB)]
        g_in, squares, ready, order_s = sem("gf_in"), sem("squares_f"), sem("ready_f"), sem("order_f")
        with nc.Block() as block:

            @block.sync
            def _(sp):
                for b in range(TB):
                    sp.dma_start(x2[:, b, :], rows.x1[b * P:(b + 1) * P, :]).then_inc(x_in[b], 16)
                for b in range(TB):
                    sp.wait_ge(ready, b + 1)
                    sp.dma_start(out[0, b * P:(b + 1) * P, :], y2[:, b, :]).then_inc(st[b], 16)
                for b in range(TB):
                    sp.wait_ge(st[b], 16)

            @block.scalar
            def _(act):
                act.dma_start(g[:, :], d["final_g"].partition_broadcast(P)).then_inc(g_in, 16)
                for b in range(TB):
                    act.wait_ge(x_in[b], 16)
                    if b:
                        act.wait_ge(squares, b)
                    act.activation(junk[:, :], x2[:, b, :], ACT.Square, accum_out=ss[:, b:b + 1]).then_inc(squares, 1)

            @block.vector
            def _(dve):
                o = Order(dve, order_s)
                dve.wait_ge(g_in, 16)
                for half in range(4):
                    dve.wait_ge(squares, 2 * (half + 1))
                    c = slice(2 * half, 2 * half + 2)
                    rsqrt_mean(dve, o, rstd[:, c], ss[:, c], tmp[:, :, c], D)
                    o.need()
                    for b in range(2 * half, 2 * half + 2):
                        dve.scalar_tensor_tensor(y2[:, b, :], x2[:, b, :], rstd[:, b:b + 1], g[:, :], ALU.mult,
                                                 ALU.mult).then_inc(ready, 1)


class Rows:

    def __init__(self, nc):
        self.x1 = nc.dram_tensor("x1_rows", (ROWS, D), F32, kind="Internal").ap()
        self.h2 = nc.dram_tensor("h2_rows", (ROWS, D), F32, kind="Internal").ap()
        self.meta = nc.dram_tensor("meta_rows", (3, P), I32, kind="Internal").ap()


class Kept:

    def __init__(self, sb):
        self.ident = sb("ident", [P, P])
        self.logits = sb("logits", [P, TB, E])


class Routes:

    def __init__(self, sb):
        self.slot = sb("slot", [P, TB, E])
        self.gate = sb("gate", [P, TB, E])
        self.bias = sb("bias", [P, 3, KC, E])
        self.iota = sb("iota_slots", [P, SLOTS])
        self.pad = sb("pad_rows", [P, 2])
        self.tok_gate = sb("tok_gate", [P, TB, 2])
        self.meta = sb("meta", [1, 3, P + 1], I32)


def build(nc, d, out):
    rows = Rows(nc)
    with ExitStack() as ctx:
        sb = lambda name, shape, dt=F32: ctx.enter_context(nc.sbuf_tensor(name, shape, dt))
        keep = Kept(sb)
        mixer(nc, d, keep, rows)
        r = Routes(sb)
        routing(nc, d, keep, rows, r)
        experts(nc, d, keep, rows, r)
        final(nc, d, keep, rows, out)


INPUTS = ["x", "norm1_g", "w_in", "lambda_q1", "lambda_k1", "lambda_q2", "lambda_k2", "subln_g", "w_pool", "b_pool",
          "pool_scale", "w_out", "norm2_g", "router_w", "router_b", "w_gate", "b_gate", "w_up", "b_up", "w_down",
          "b_down", "final_g"]


def kernel(**inputs):
    import concourse.bacc as bacc
    from concourse.bass_utils import run_bass_kernel_spmd

    nc = bacc.Bacc("TRN2", target_bir_lowering=False, num_devices=1)
    arrays, d = {}, {}
    for name in INPUTS:
        a = np.ascontiguousarray(inputs[name])
        arrays["in_" + name] = a
        d[name] = nc.dram_tensor("in_" + name, a.shape, mybir.dt.from_np(a.dtype), kind="ExternalInput").ap()
    out = nc.dram_tensor("out", (1, S, D), F32, kind="ExternalOutput").ap()
    build(nc, d, out)
    r = run_bass_kernel_spmd(nc, [arrays], core_ids=[0])
    return r.results[0]["out"]
```

```python
import numpy as np
import concourse.bass as bass
import concourse.mybir as mybir
from concourse.alu_op_type import AluOpType as ALU
from contextlib import ExitStack

ACT = mybir.ActivationFunctionType
AX = mybir.AxisListType.X
F32, BF16, I32, U32 = mybir.dt.float32, mybir.dt.bfloat16, mybir.dt.int32, mybir.dt.uint32

P = 128
S, D = 1024, 1024
TB, KC = S // P, D // P
D_ATTN, HEADS, DQK, DV = 512, 4, 64, 128
POOLS = 4
WMAX = 2 ** POOLS
LAMBDA_INIT = 0.8 - 0.6
EPS = 1e-5
E, TOPK = 32, 4
LIMIT, ALPHA = 7.0, 1.702
HALF = 512
SLOTS = 256
ITEMS = (S * TOPK + E * (SLOTS - 1)) // SLOTS
LEVELS = (96, 112, 120, 128, 136, 144, 152, 160, 176, 192, 224, 256)
ONE_HALF = sum(n <= P for n in LEVELS)
PAD = SLOTS
ROWS = S + PAD
GROUPS = 6
MASKED = -1e30
MAGIC = 0x5F3759DF


class Order:

    def __init__(self, eng, sem, base=0):
        self.eng, self.sem, self.n, self.base = eng, sem, 0, base

    def did(self, ins):
        self.n += 1
        ins.then_inc(self.sem, 1)

    def need(self):
        if isinstance(self.base, int) and not self.base + self.n:
            return
        self.eng.wait_ge(self.sem, self.base + self.n)


def bcast(ap, n):
    return ap.unsqueeze(2).broadcast_to([ap.shape[0], ap.shape[1], n])


def repeat(ap, n):
    return ap.unsqueeze(1).broadcast_to([ap.shape[0], n, ap.shape[1]])


def rsqrt_mean(eng, order, out, sums, tmp, n, extra=1.0):
    v, t, y = tmp[:, 0], tmp[:, 1], tmp[:, 2]
    order.need()
    order.did(eng.tensor_scalar(v, sums, 1.0 / n, EPS, ALU.mult, ALU.add))
    order.need()
    order.did(eng.tensor_scalar(y.bitcast(I32), v.bitcast(I32), -0.5, float(MAGIC), ALU.mult, ALU.add))
    for step in range(3):
        order.need()
        order.did(eng.tensor_tensor(t, y, y, ALU.mult))
        order.need()
        order.did(eng.tensor_tensor(t, t, v, ALU.mult))
        order.need()
        order.did(eng.tensor_scalar(t, t, -0.5, 1.5, ALU.mult, ALU.add))
        order.need()
        order.did(eng.tensor_tensor(y, y, t, ALU.mult))
    order.need()
    order.did(eng.tensor_scalar(out, y, float(extra), None, ALU.mult))


def mixer(nc, d, keep, rows):
    with ExitStack() as ctx:
        sb = lambda name, shape, dt=F32: ctx.enter_context(nc.sbuf_tensor(name, shape, dt))
        sem = lambda name: ctx.enter_context(nc.semaphore(name))
        ps = ctx.enter_context(nc.psum_tensor("ps_mixer", [P, 8, HALF], F32))
        x = sb("x", [P, TB, D])
        xn = sb("xn", [P, TB, D])
        hT = sb("hT", [P, KC, S])
        qkT = sb("qkT", [P, 2, HEADS, S])
        v = sb("v", [P, TB, D_ATTN])
        uT = sb("uT", [P, POOLS, S])
        ring = sb("w_ring", [P, 2, KC, HALF])
        g2 = sb("g2", [P, D])
        mask = sb("mask", [P, P])
        wp = sb("wp", [P, POOLS, P])
        rw = sb("rw", [P, KC, E])
        rb = sb("rb", [P, E])
        vec_rows = sb("vec_rows", [17, P])
        vec = sb("vec", [P, 17])
        lam_in = sb("lam_in", [P, 4, DQK])
        lam = sb("lam", [P, 8])
        ss = sb("ss", [P, TB])
        rstd = sb("rstd", [P, TB])
        tmp = sb("tmp", [P, 3, TB])
        inv_i = sb("inv_i", [P, WMAX], I32)
        inv = sb("inv", [P, 5, WMAX])
        o_rms = sb("o_rms", [P, 5, HEADS])
        soft = sb("soft", [P, 8, 2])
        r0 = sb("r0", [P, 2, HEADS])
        ident = keep.ident
        junk = uT[:, 3]
        pool_a, pool_b = xn[:, 0], xn[:, 1]
        probs = xn[:, 2:6]
        comb = xn[:, 6:8]
        combT = [a.rearrange("p (k t) -> p k t", t=P) for a in (xn[:, 1], uT[:, 0])]
        ot = xn[:, 0, HALF:D]
        o4 = ot.rearrange("p (h t) -> p h t", h=HEADS)
        o_sq = xn[:, 0, 0:HALF].rearrange("p (h t) -> p h t", h=HEADS)
        mixT, h2T = hT, qkT.rearrange("p a h s -> p (a h) s")
        g_in = vec[:, 0:8]
        b_pool, s_pool, g_sub = vec[:, 8:12], vec[:, 12:16], vec[:, 16:17]

        x_in = [sem(f"x_in{b}") for b in range(TB)]
        vec_in, lam_ld, g2_in, wp_in, rw_in, rb_in = (sem(n) for n in ("vec_in", "lam_ld", "g2_in", "wp_in", "rw_in", "rb_in"))
        w_in = [sem(f"w_in{i}") for i in range(6)]
        zeroed, zero_st = sem("zeroed"), [sem(f"zero_st{i}") for i in range(4)]
        consts, squares, normed, vec_ready = sem("consts"), sem("squares"), sem("normed"), sem("vec_ready")
        vec_mm, job_done, lam_exp = sem("vec_mm"), sem("job_done"), sem("lam_exp")
        ev = {"act": sem("ev_act"), "dve": sem("ev_dve")}
        order_s, pool_s, lam_s = sem("order_s"), sem("pool_s"), sem("lam_s")
        pooled = sem("pooled")
        scored, biased, exped, combined = sem("scored"), sem("biased"), sem("exped"), sem("combined")
        turned, turn_ev, o_done, o_out, o_norm, oT_done, mixed = (sem(n) for n in ("turned", "turn_ev", "o_done", "o_out", "o_norm", "oT_done", "mixed"))
        x1_ready, h2_ready, sq2 = (sem(n) for n in ("x1_ready", "h2_ready", "sq2"))
        st = [sem(f"st{i}") for i in range(2 * TB)]

        jobs = [("norm", q, k, "act" if k % 2 else "dve") for q in range(2) for k in range(KC)]
        jobs += [(w, h, q, "act" if q else "dve") for w in ("q", "k", "u") for h in range(4) for q in range(2)]
        jobs += [("v", b, 0, "act") for b in range(TB)]
        jobs += [("pool", g, q, "dve") for g in range(POOLS) for q in range(2)]
        first_out = len(jobs)
        outs = [("out", b, n, "dve") for b in range(TB) for n in range(2)]
        norm2 = [[("norm2", q, k, "act" if k % 2 else "dve") for k in range(KC)] for q in range(2)]
        router = [("router", q, 0, "dve") for q in range(2)]
        jobs += outs[:12] + norm2[0] + outs[12:] + router[:1] + norm2[1] + router[1:]
        tile_of = {"q": 0, "k": 1, "u": 2, "v": 3}

        def emptied(n):
            who = jobs[n][3]
            return who, sum(j[3] == who for j in jobs[:n + 1])

        units = [(i, h) for i in range(TB) for h in range(HEADS)]
        turns = [sum(-(-(i + 1) // 4) for i, h in units[:u]) for u in range(len(units) + 1)]

        with nc.Block() as block:

            @block.sync
            def _(sp):
                sp.dma_start(vec_rows[0:8, :], d["norm1_g"].rearrange("a (k p) -> (a k) p", p=P)).then_inc(vec_in, 16)
                sp.dma_start(vec_rows[8:12, :], d["b_pool"].rearrange("a g p -> (a g) p")).then_inc(vec_in, 16)
                sp.dma_start(vec_rows[12:16, :], d["pool_scale"].rearrange("a (g p) -> (a g) p", p=P)).then_inc(vec_in, 16)
                sp.dma_start(vec_rows[16:17, :], d["subln_g"]).then_inc(vec_in, 16)
                for b in range(TB):
                    sp.dma_start(x[:, b, :], d["x"][0, b * P:(b + 1) * P, :]).then_inc(x_in[b], 16)
                for t, c in enumerate((0, 1, 3, 2)):
                    if t >= 2:
                        sp.wait_ge(job_done, 16 + 8 * (t - 1))
                    sp.dma_start(ring[:, t % 2], d["w_in"][0, :, c * HALF:(c + 1) * HALF].rearrange(
                        "(k p) n -> p k n", p=P)).then_inc(w_in[t], 16)
                for n in range(2):
                    sp.wait_ge(job_done, 16 + 8 * (n + 3))
                    sp.dma_start(ring[:, n], d["w_out"][0, :, n * HALF:(n + 1) * HALF].rearrange(
                        "(k p) n -> p k n", p=P)).then_inc(w_in[4 + n], 16)
                for b in range(TB):
                    sp.wait_ge(x1_ready, 2 * (b + 1))
                    sp.dma_start(rows.x1[b * P:(b + 1) * P, :], x[:, b, :]).then_inc(st[b], 16)
                for b in range(TB):
                    sp.wait_ge(h2_ready, b + 1)
                    sp.dma_start(rows.h2[b * P:(b + 1) * P, :], xn[:, b, :]).then_inc(st[TB + b], 16)
                for s in st:
                    sp.wait_ge(s, 16)

            @block.gpsimd
            def _(pool):
                pool.memset(ident[:, :], 0.0).then_inc(consts, 1)
                pool.memset(mask[:, :], 0.0).then_inc(consts, 1)
                pool.iota(inv_i[:, :], [[1, WMAX]], base=1, channel_multiplier=0).then_inc(consts, 1)
                pool.memset(hT[:, 0, :], 0.0).then_inc(zeroed, 1)
                pool.wait_ge(consts, 3)
                pool.affine_select(out=ident[:, :], in_=ident[:, :], compare_op=ALU.not_equal, fill=1.0,
                                   base=0, pattern=[[-1, P]], channel_multiplier=1).then_inc(consts, 1)
                pool.affine_select(out=mask[:, :], in_=mask[:, :], compare_op=ALU.is_ge, fill=MASKED,
                                   base=0, pattern=[[-1, P]], channel_multiplier=1).then_inc(consts, 1)
                pool.wait_ge(zeroed, 1)
                for i, dst in enumerate((rows.x1, rows.h2)):
                    for r in range(PAD // P):
                        z = 2 * i + r
                        pool.dma_start(dst[S + r * P:S + (r + 1) * P, :], hT[:, 0, :]).then_inc(zero_st[z], 16)
                for z in zero_st:
                    pool.wait_ge(z, 16)
                pool.sem_inc(zeroed, 1)
                o = Order(pool, pool_s)
                for i in range(TB):
                    pool.wait_ge(o_out, i + 1)
                    o.did(pool.tensor_tensor(o_sq, o4, o4, ALU.mult))
                    w = DV // 2
                    while w:
                        o.need()
                        o.did(pool.tensor_tensor(o_sq[:, :, 0:w], o_sq[:, :, 0:w], o_sq[:, :, w:2 * w], ALU.add))
                        w //= 2
                    rsqrt_mean(pool, o, o_rms[:, 1, :].unsqueeze(2), o_sq[:, :, 0:1], o_rms[:, 2:5].unsqueeze(3), DV)
                    o.need()
                    pool.tensor_tensor(o4, o4, bcast(o_rms[:, 1], P), ALU.mult).then_inc(o_norm, 1)

            @block.scalar
            def _(act):
                act.dma_start(lam_in[:, 0, :], d["lambda_q1"].partition_broadcast(P)).then_inc(lam_ld, 16)
                act.dma_start(lam_in[:, 1, :], d["lambda_q2"].partition_broadcast(P)).then_inc(lam_ld, 16)
                act.dma_start(lam_in[:, 2, :], d["lambda_k1"].partition_broadcast(P)).then_inc(lam_ld, 16)
                act.dma_start(lam_in[:, 3, :], d["lambda_k2"].partition_broadcast(P)).then_inc(lam_ld, 16)
                act.dma_start(wp[:, :, :], d["w_pool"][0].rearrange("g c n -> c g n")).then_inc(wp_in, 16)
                act.dma_start(rw[:, :, :], d["router_w"][0].rearrange("(k p) e -> p k e", p=P)).then_inc(rw_in, 16)
                act.dma_start(rb[:, :], d["router_b"].partition_broadcast(P)).then_inc(rb_in, 16)
                act.dma_start(g2[:, :], d["norm2_g"].partition_broadcast(P)).then_inc(g2_in, 16)
                for b in range(TB):
                    act.wait_ge(x_in[b], 16)
                    if b:
                        act.wait_ge(squares, b)
                    act.activation(junk, x[:, b, :], ACT.Square, accum_out=ss[:, b:b + 1]).then_inc(squares, 1)
                act.wait_ge(lam_s, 2)
                act.activation(lam[:, 2:4], lam[:, 0:2], ACT.Exp).then_inc(lam_exp, 1)

                def empty(n):
                    what, a, b, who = jobs[n]
                    if who != "act":
                        return
                    act.wait_ge(job_done, n + 1)
                    bank = ps[:, n % 8, :]
                    if what == "norm":
                        if n == 1:
                            act.wait_ge(vec_ready, 1)
                            act.wait_ge(zeroed, 2)
                        ins = act.activation(hT[:, b, a * HALF:(a + 1) * HALF], bank, ACT.Copy, scale=g_in[:, b:b + 1])
                    elif what in "qk":
                        ins = act.activation(qkT[:, "qk".index(what), a, b * HALF:(b + 1) * HALF], bank, ACT.Copy)
                    elif what == "u":
                        ins = act.activation(uT[:, a, b * HALF:(b + 1) * HALF], bank, ACT.Copy)
                    elif what == "v":
                        ins = act.activation(v[:, a, :], bank, ACT.Copy)
                    else:
                        ins = act.activation(h2T[:, b, a * HALF:(a + 1) * HALF], bank, ACT.Copy)
                    ins.then_inc(ev["act"], 1)

                for n in range(first_out):
                    empty(n)

                def exps(step):
                    u, m = divmod(step, 2)
                    i, h = units[u]
                    act.wait_ge(biased, step + 1)
                    if u >= 2:
                        act.wait_ge(combined, u - 1)
                    n = (i + 1) * P
                    s4 = step % 4
                    act.activation(probs[:, s4, 0:n], ps[:, 2 * m:2 * m + 2, :].rearrange("p a b -> p (a b)")[:, 0:n],
                                   ACT.Exp, bias=soft[:, s4, 0:1], scale=DQK ** -0.5,
                                   accum_out=soft[:, s4, 1:2]).then_inc(exped, 1)

                def leave(u):
                    i, h = units[u]
                    for t in range(0, i + 1, 4):
                        w, tb = min(4, i + 1 - t), turns[u] + t // 4
                        act.wait_ge(turned, tb + 1)
                        act.activation(combT[u % 2][:, t:t + w, :], ps[:, 4 + tb % 2, 0:w * P].rearrange(
                            "p (a b) -> p a b", b=P), ACT.Copy).then_inc(turn_ev, 1)

                def mix(i):
                    act.wait_ge(oT_done, i + 1)
                    act.activation(mixT[:, 0:HEADS, i * P:(i + 1) * P], ps[:, 6 + i % 2, :].rearrange(
                        "p (h t) -> p h t", h=HEADS), ACT.Copy, scale=g_sub).then_inc(mixed, 1)

                exps(0)
                exps(1)
                for u, (i, h) in enumerate(units):
                    if u + 1 < len(units):
                        exps(2 * u + 2)
                        exps(2 * u + 3)
                    leave(u)
                    if h == HEADS - 1 and i >= 1:
                        mix(i - 1)
                mix(TB - 1)
                for q in range(2):
                    for b in range(4 * q, 4 * q + 4):
                        act.wait_ge(x1_ready, 2 * (b + 1))
                        if b:
                            act.wait_ge(sq2, b)
                        act.activation(junk, x[:, b, :], ACT.Square, accum_out=ss[:, b:b + 1]).then_inc(sq2, 1)
                    for n, job in enumerate(jobs):
                        if job[:2] == ("norm2", q):
                            empty(n)

            @block.vector
            def _(dve):
                o = Order(dve, order_s)
                dve.wait_ge(lam_ld, 64)
                dve.tensor_tensor(lam_in[:, 0:2, :], lam_in[:, 0:2, :], lam_in[:, 2:4, :], ALU.mult).then_inc(lam_s, 1)
                dve.wait_ge(lam_s, 1)
                dve.reduce_sum(lam[:, 0:2], lam_in[:, 0:2, :], axis=AX).then_inc(lam_s, 1)
                dve.wait_ge(vec_mm, 1)
                o.did(dve.tensor_copy(vec[:, :], ps[:, 7, 0:17]))
                o.need()
                dve.tensor_scalar(g_sub, g_sub, 1.0 - LAMBDA_INIT, None, ALU.mult).then_inc(vec_ready, 1)
                dve.wait_ge(consts, 5)
                o.did(dve.tensor_copy(inv[:, 4, :], inv_i[:, :]))
                o.need()
                o.did(dve.reciprocal(inv[:, 4, :], inv[:, 4, :]))
                o.need()
                for g in range(POOLS):
                    o.did(dve.tensor_scalar(inv[:, g, :], inv[:, 4, :], 1.0 / 2 ** (g + 1), None, ALU.max))
                for first, end in ((0, 2), (2, 4), (4, 8)):
                    dve.wait_ge(squares, end)
                    c = slice(first, end)
                    rsqrt_mean(dve, o, rstd[:, c], ss[:, c], tmp[:, :, c], D)
                    o.need()
                    for b in range(first, end):
                        dve.tensor_scalar(xn[:, b, :], x[:, b, :], rstd[:, b:b + 1], None, ALU.mult).then_inc(normed, 1)
                dve.wait_ge(lam_exp, 1)
                o.did(dve.tensor_tensor(lam[:, 4:5], lam[:, 3:4], lam[:, 2:3], ALU.subtract))
                o.need()
                o.did(dve.tensor_scalar(lam[:, 5:6], lam[:, 4:5], -LAMBDA_INIT, None, ALU.add))
                neg_lam = lam[:, 5:6]

                def empty(n):
                    what, a, b, who = jobs[n]
                    if who != "dve":
                        return
                    dve.wait_ge(job_done, n + 1)
                    bank = ps[:, n % 8, :]
                    if what == "norm":
                        if n == 0:
                            dve.wait_ge(vec_ready, 1)
                            dve.wait_ge(zeroed, 2)
                        ins = dve.tensor_scalar(hT[:, b, a * HALF:(a + 1) * HALF], bank, g_in[:, b:b + 1], None, ALU.mult)
                    elif what in "qk":
                        ins = dve.tensor_copy(qkT[:, "qk".index(what), a, b * HALF:(b + 1) * HALF], bank)
                    elif what == "u":
                        ins = dve.tensor_copy(uT[:, a, b * HALF:(b + 1) * HALF], bank)
                    elif what == "pool":
                        if a == 0 and b == 0:
                            dve.wait_ge(job_done, 48)
                        ins = dve.tensor_scalar(mixT[:, 4 + a, b * HALF:(b + 1) * HALF], bank, b_pool[:, a:a + 1],
                                                s_pool[:, a:a + 1], ALU.add, ALU.mult)
                    elif what == "out":
                        xs = x[:, a, b * HALF:(b + 1) * HALF]
                        dve.tensor_tensor(xs, bank, xs, ALU.add).then_inc(x1_ready, 1)
                        return
                    elif what == "router":
                        dve.wait_ge(rb_in, 16)
                        ins = dve.tensor_tensor(keep.logits[:, 4 * a:4 * a + 4, :], bank[:, 0:4 * E].rearrange("p (b e) -> p b e", e=E),
                                                repeat(rb[:, :], 4), ALU.add)
                    else:
                        ins = dve.tensor_copy(h2T[:, b, a * HALF:(a + 1) * HALF], bank)
                    ins.then_inc(ev["dve"], 1)

                for n in range(first_out - 8):
                    empty(n)
                dve.wait_ge(ev["act"], emptied(39)[1])
                dve.wait_ge(ev["dve"], emptied(38)[1])
                for g in range(POOLS):
                    src = uT[:, g, :]
                    if g:
                        dve.wait_ge(pooled, g)
                    for i in range(g + 1):
                        dst, w = (pool_a, pool_b)[i % 2], 2 ** i
                        o.need()
                        o.did(dve.tensor_tensor(dst[:, w:S], src[:, w:S], src[:, 0:S - w], ALU.add))
                        o.did(dve.tensor_copy(dst[:, 0:w], src[:, 0:w]))
                        src = dst
                    o.need()
                    o.did(dve.tensor_tensor(src[:, 0:WMAX], src[:, 0:WMAX], inv[:, g, :], ALU.mult))
                    o.need()
                    o.did(dve.tensor_tensor(uT[:, g, 0:WMAX], src[:, 0:WMAX], uT[:, g, 0:WMAX], ALU.subtract))
                    dve.scalar_tensor_tensor(uT[:, g, WMAX:S], src[:, WMAX:S], 1.0 / 2 ** (g + 1), uT[:, g, WMAX:S],
                                             ALU.mult, ALU.subtract).then_inc(pooled, 1)
                for n in range(first_out - 8, first_out):
                    empty(n)

                def bias(step):
                    u, m = divmod(step, 2)
                    i, h = units[u]
                    s4, n = step % 4, (i + 1) * P
                    sc = ps[:, 2 * m:2 * m + 2, :].rearrange("p a b -> p (a b)")
                    dve.wait_ge(scored, step + 1)
                    o.did(dve.tensor_tensor(sc[:, n - P:n], sc[:, n - P:n], mask[:, :], ALU.add))
                    o.need()
                    o.did(dve.reduce_max(soft[:, 4 + s4, 0:1], sc[:, 0:n], axis=AX))
                    o.need()
                    dve.tensor_scalar(soft[:, s4, 0:1], soft[:, 4 + s4, 0:1], -DQK ** -0.5, None, ALU.mult).then_inc(biased, 1)

                def combine(u):
                    i, h = units[u]
                    n, a, b = (i + 1) * P, (2 * u) % 4, (2 * u + 1) % 4
                    dve.wait_ge(exped, 2 * u + 2)
                    o.did(dve.reciprocal(r0[:, i % 2, h:h + 1], soft[:, a, 1:2]))
                    o.did(dve.reciprocal(soft[:, 4 + b, 1:2], soft[:, b, 1:2]))
                    o.need()
                    o.did(dve.scalar_tensor_tensor(soft[:, 4 + a, 1:2], soft[:, a, 1:2], soft[:, 4 + b, 1:2], neg_lam,
                                                   ALU.mult, ALU.mult))
                    o.need()
                    if u >= 2:
                        dve.wait_ge(turned, turns[u - 1])
                    dve.scalar_tensor_tensor(comb[:, u % 2, 0:n], probs[:, b, 0:n], soft[:, 4 + a, 1:2],
                                             probs[:, a, 0:n], ALU.mult, ALU.add).then_inc(combined, 1)

                def take_out(i):
                    dve.wait_ge(o_done, i + 1)
                    if i:
                        dve.wait_ge(oT_done, i)
                    dve.tensor_tensor(o4, ps[:, 6 + i % 2, :].rearrange("p (h t) -> p h t", h=HEADS),
                                      bcast(r0[:, i % 2, :], P), ALU.mult).then_inc(o_out, 1)

                bias(0)
                bias(1)
                for u, (i, h) in enumerate(units):
                    combine(u)
                    if u + 1 < len(units):
                        bias(2 * u + 2)
                        bias(2 * u + 3)
                    if h == 1 and i >= 1:
                        take_out(i - 1)
                take_out(TB - 1)

                def norm_two(pair):
                    c = slice(2 * pair, 2 * pair + 2)
                    dve.wait_ge(sq2, 2 * pair + 2)
                    rsqrt_mean(dve, o, rstd[:, c], ss[:, c], tmp[:, :, c], D)
                    o.need()
                    for b in range(2 * pair, 2 * pair + 2):
                        dve.scalar_tensor_tensor(xn[:, b, :], x[:, b, :], rstd[:, b:b + 1], g2[:, :], ALU.mult,
                                                 ALU.mult).then_inc(h2_ready, 1)

                for n in range(first_out, len(jobs)):
                    what, a, b, _ = jobs[n]
                    if n == first_out:
                        dve.wait_ge(g2_in, 16)
                    if (what, a) == ("router", 0):
                        norm_two(3)
                    empty(n)
                    if (what, b) == ("out", 1) and a in (2, 4, 6):
                        norm_two(a // 2 - 1)
                dve.wait_ge(ev["dve"], sum(j[3] == "dve" and j[0] != "out" for j in jobs))

            @block.tensor
            def _(pe):
                pe.wait_ge(consts, 5)
                pe.wait_ge(vec_in, 64)
                pe.transpose(ps[:, 7, 0:17], vec_rows[:, :], ident[0:17, 0:17]).then_inc(vec_mm, 1)
                pe.wait_ge(vec_ready, 1)

                def bank_for(n):
                    if n >= 8 and n != first_out:
                        if jobs[n - 8][0] == "out":
                            pe.wait_ge(x1_ready, sum(j[0] == "out" for j in jobs[:n - 7]))
                        elif n - 8 < first_out <= n:
                            pass
                        else:
                            who, count = emptied_no_out(n - 8)
                            pe.wait_ge(ev[who], count)
                    return ps[:, n % 8, :]

                def emptied_no_out(n):
                    who = jobs[n][3]
                    return who, sum(j[3] == who and j[0] != "out" for j in jobs[:n + 1])

                for n in range(first_out):
                    what, a, b, _ = jobs[n]
                    if what in tile_of and (a, b) == (0, 0):
                        pe.wait_ge(w_in[tile_of[what]], 16)
                        if what == "q":
                            pe.wait_ge(ev["act"], 8)
                            pe.wait_ge(ev["dve"], 8)
                    bank = bank_for(n)
                    if what == "norm":
                        for t in range(4):
                            pe.wait_ge(normed, 4 * a + t + 1)
                            ins = pe.transpose(bank[:, t * P:(t + 1) * P], xn[:, 4 * a + t, b * P:(b + 1) * P], ident[:, :])
                    elif what == "v":
                        for k in range(KC):
                            ins = pe.matmul(bank, hT[:, k, a * P:(a + 1) * P], ring[:, 1, k, :], start=k == 0, stop=k == KC - 1)
                    elif what == "pool":
                        pe.wait_ge(wp_in, 16)
                        pe.wait_ge(pooled, a + 1)
                        ins = pe.matmul(bank, wp[:, a, :], uT[:, a, b * HALF:(b + 1) * HALF], start=True, stop=True)
                    else:
                        for k in range(KC):
                            ins = pe.matmul(bank, ring[:, tile_of[what] % 2, k, a * P:(a + 1) * P],
                                            hT[:, k, b * HALF:(b + 1) * HALF], start=k == 0, stop=k == KC - 1)
                    ins.then_inc(job_done, 1)
                pe.wait_ge(ev["dve"], emptied_no_out(first_out - 1)[1])
                pe.wait_ge(ev["act"], sum(j[3] == "act" for j in jobs[:first_out]))

                def scores(step):
                    u, m = divmod(step, 2)
                    i, h = units[u]
                    if step >= 2:
                        pe.wait_ge(exped, step - 1)
                    part = slice(m * DQK, (m + 1) * DQK)
                    for c in range(0, (i + 1) * P, HALF):
                        w = min(HALF, (i + 1) * P - c)
                        ins = pe.matmul(ps[:, 2 * m + c // HALF, 0:w], qkT[part, 0, h, i * P:(i + 1) * P],
                                        qkT[part, 1, h, c:c + w], start=True, stop=True)
                    ins.then_inc(scored, 1)

                def turn_out(i):
                    pe.wait_ge(o_norm, i + 1)
                    for h in range(HEADS):
                        ins = pe.transpose(ps[:, 6 + i % 2, h * P:(h + 1) * P], ot[:, h * P:(h + 1) * P], ident[:, :])
                    ins.then_inc(oT_done, 1)

                def turn(u):
                    i, h = units[u]
                    pe.wait_ge(combined, u + 1)
                    for t in range(0, i + 1, 4):
                        tb = turns[u] + t // 4
                        if tb >= 2:
                            pe.wait_ge(turn_ev, tb - 1)
                        for k in range(t, min(t + 4, i + 1)):
                            ins = pe.transpose(ps[:, 4 + tb % 2, (k - t) * P:(k - t + 1) * P],
                                               comb[:, u % 2, k * P:(k + 1) * P], ident[:, :])
                        ins.then_inc(turned, 1)

                def values(u):
                    i, h = units[u]
                    pe.wait_ge(turn_ev, turns[u + 1])
                    if h == 0 and i >= 2:
                        pe.wait_ge(mixed, i - 1)
                    for k in range(i + 1):
                        ins = pe.matmul(ps[:, 6 + i % 2, h * P:(h + 1) * P], combT[u % 2][:, k, :], v[:, k, h * P:(h + 1) * P],
                                        start=k == 0, stop=k == i)
                    if h == HEADS - 1:
                        ins.then_inc(o_done, 1)

                scores(0)
                scores(1)
                for u, (i, h) in enumerate(units):
                    if u + 1 < len(units):
                        scores(2 * u + 2)
                        scores(2 * u + 3)
                    turn(u)
                    if h == HEADS - 1 and i >= 1:
                        turn_out(i - 1)
                    if u:
                        values(u - 1)
                values(len(units) - 1)
                pe.wait_ge(mixed, TB - 1)
                pe.wait_ge(w_in[4], 16)
                pe.wait_ge(w_in[5], 16)
                for n in range(first_out, len(jobs)):
                    what, a, b, _ = jobs[n]
                    if n == first_out + 4:
                        turn_out(TB - 1)
                        pe.wait_ge(mixed, TB)
                    bank = bank_for(n)
                    if what == "out":
                        for k in range(KC):
                            ins = pe.matmul(bank, mixT[:, k, a * P:(a + 1) * P], ring[:, b, k, :], start=k == 0, stop=k == KC - 1)
                    elif what == "router":
                        last = max(m for m in range(n) if jobs[m][:2] == ("norm2", a))
                        pe.wait_ge(ev["dve"], emptied_no_out(last - 1)[1])
                        pe.wait_ge(ev["act"], emptied_no_out(last)[1])
                        pe.wait_ge(rw_in, 16)
                        for t in range(4):
                            for k in range(KC):
                                ins = pe.matmul(bank[:, t * E:(t + 1) * E], h2T[:, k, (4 * a + t) * P:(4 * a + t + 1) * P],
                                                rw[:, k, :], start=k == 0, stop=k == KC - 1)
                    else:
                        for t in range(4):
                            pe.wait_ge(h2_ready, 4 * a + t + 1)
                            ins = pe.transpose(bank[:, t * P:(t + 1) * P], xn[:, 4 * a + t, b * P:(b + 1) * P], ident[:, :])
                    ins.then_inc(job_done, 1)


def routing(nc, d, keep, rows, r):
    with ExitStack() as ctx:
        sb = lambda name, shape, dt=F32: ctx.enter_context(nc.sbuf_tensor(name, shape, dt))
        sem = lambda name: ctx.enter_context(nc.semaphore(name))
        ps = ctx.enter_context(nc.psum_tensor("ps_routing", [P, 4, HALF], F32))
        tri, ones = sb("tri", [P, P]), sb("ones", [P, P])
        iota_i, iota_e = sb("iota_i", [P, SLOTS], I32), sb("iota_e", [P, E])
        small_i, small = sb("small_i", [P, 4 + 2 * TB], I32), sb("small", [P, 4])
        bias_rows = sb("bias_rows", [E, 3, D])
        top, where = sb("top", [P, TB, 8]), sb("where", [P, TB, 8], U32)
        where_f, gates = sb("where_f", [P, TB, 8]), sb("gates", [P, TB, TOPK])
        total = sb("total", [P, TB])
        hit, member = sb("hit", [P, TB, E]), sb("member", [P, TB, E])
        gate = sb("gate_f32", [P, TB, E])
        off = sb("off", [P, TB + 1, E])
        blocks, ends, starts = sb("blocks", [P, E]), sb("ends", [P, E]), sb("starts", [P, E])
        ones_e, hit_e, prod = sb("ones_e", [P, E]), sb("hit_e", [P, E]), sb("prod", [P, E])
        item = sb("item", [P, 8])
        steps, above = sb("steps", [P, len(LEVELS) - 1]), sb("above", [P, len(LEVELS) - 1])
        meta_i = sb("meta_i", [P, 4], I32)
        made, biases_in, topped, exped = sem("made"), sem("biases_in"), sem("topped"), sem("exped_g")
        order_s, member_ready, rank_mm, bias_mm, meta_ready = (sem(n) for n in ("order_r", "member_ready", "rank_mm", "bias_mm", "meta_ready"))
        meta_st, meta_ld = sem("meta_st"), sem("meta_ld")

        with nc.Block() as block:

            @block.gpsimd
            def _(pool):
                pool.memset(tri[:, :], 1.0).then_inc(made, 1)
                pool.memset(ones[:, :], 1.0).then_inc(made, 1)
                pool.memset(ones_e[:, :], 1.0).then_inc(made, 1)
                pool.iota(iota_i[:, :], [[1, SLOTS]], base=0, channel_multiplier=0).then_inc(made, 1)
                pool.iota(small_i[:, 0:1], [[0, 1]], base=0, channel_multiplier=1).then_inc(made, 1)
                pool.iota(small_i[:, 1:3], [[P, 2]], base=S + 1, channel_multiplier=1).then_inc(made, 1)
                by_block = small_i[:, 4:4 + 2 * TB].rearrange("p (b c) -> p b c", c=2)
                pool.iota(by_block[:, :, 0], [[P, TB]], base=0, channel_multiplier=0).then_inc(made, 1)
                pool.iota(by_block[:, :, 1], [[0, TB]], base=1, channel_multiplier=1).then_inc(made, 1)
                pool.memset(small_i[:, 3:4], 0).then_inc(made, 1)
                pool.memset(r.meta[:, :, :], 0).then_inc(made, 1)
                for i, n in enumerate(LEVELS[:-1]):
                    pool.memset(steps[:, i:i + 1], float(n)).then_inc(made, 1)
                pool.wait_ge(made, 10 + len(LEVELS) - 1)
                pool.affine_select(out=tri[:, :], in_=tri[:, :], compare_op=ALU.is_ge, fill=0.0, base=-1,
                                   pattern=[[1, P]], channel_multiplier=-1).then_inc(made, 1)

            @block.sync
            def _(sp):
                for i, b in enumerate((d["b_gate"], d["b_up"], d["b_down"])):
                    sp.dma_start(bias_rows[:, i, :], b[0]).then_inc(biases_in, 16)
                sp.wait_ge(meta_ready, 1)
                with nc.allow_non_contiguous_dma("a column becomes a row"):
                    sp.dma_start(rows.meta.rearrange("a p -> p a"), meta_i[:, 0:3]).then_inc(meta_st, 16)
                sp.wait_ge(meta_st, 16)
                sp.dma_start(r.meta[0:1, :, 1:1 + P], rows.meta.rearrange("(o a) p -> o a p", o=1)).then_inc(meta_ld, 16)
                sp.wait_ge(meta_ld, 16)

            @block.scalar
            def _(act):
                act.wait_ge(topped, 1)
                act.activation(gates[:, :, :], gates[:, :, :], ACT.Exp).then_inc(exped, 1)

            @block.tensor
            def _(pe):
                pe.wait_ge(biases_in, 48)
                for i in range(3):
                    for m in range(KC):
                        ins = pe.transpose(ps[:, 2 + i // 2, ((i % 2) * KC + m) * E:((i % 2) * KC + m + 1) * E],
                                           bias_rows[:, i, m * P:(m + 1) * P], keep.ident[0:E, 0:E])
                ins.then_inc(bias_mm, 1)
                pe.wait_ge(made, 11 + len(LEVELS) - 1)
                pe.wait_ge(member_ready, 1)
                flat = member[:, :, :].rearrange("p b e -> p (b e)")
                pe.matmul(ps[:, 0, 0:TB * E], tri[:, :], flat, start=True, stop=True)
                pe.matmul(ps[:, 1, 0:TB * E], ones[:, :], flat, start=True, stop=True).then_inc(rank_mm, 1)

            @block.vector
            def _(dve):
                o = Order(dve, order_s)
                for b in range(TB):
                    o.did(dve.max(top[:, b, :], keep.logits[:, b, :]))
                o.need()
                for b in range(TB):
                    o.did(dve.max_index(where[:, b, :], top[:, b, :], keep.logits[:, b, :]))
                dve.tensor_tensor(gates[:, :, :], top[:, :, 0:TOPK], top[:, :, 0:1].broadcast_to([P, TB, TOPK]),
                                  ALU.subtract).then_inc(topped, 1)
                dve.wait_ge(made, 11 + len(LEVELS) - 1)
                o.did(dve.tensor_copy(r.iota[:, :], iota_i[:, :]))
                o.did(dve.tensor_copy(small[:, :], small_i[:, 0:4]))
                o.did(dve.tensor_copy(r.pad[:, :], small_i[:, 1:3]))
                o.did(dve.memset(r.tok_gate[:, :, :], 0.0))
                o.need()
                o.did(dve.tensor_copy(r.tok_gate[:, :, 0:2], small_i[:, 4:4 + 2 * TB].rearrange("p (b c) -> p b c", c=2)))
                o.did(dve.tensor_copy(iota_e[:, :], iota_i[:, 0:E]))
                o.need()
                o.did(dve.tensor_copy(where_f[:, :, :], where[:, :, :]))
                dve.wait_ge(exped, 1)
                o.did(dve.reduce_sum(total[:, :], gates[:, :, :], axis=AX))
                o.need()
                o.did(dve.reciprocal(total[:, :], total[:, :]))
                o.need()
                o.did(dve.tensor_tensor(gates[:, :, :], gates[:, :, :], bcast(total[:, :], TOPK), ALU.mult))
                for k in range(TOPK):
                    o.need()
                    o.did(dve.tensor_tensor(hit[:, :, :], repeat(iota_e[:, :], TB),
                                            where_f[:, :, k:k + 1].broadcast_to([P, TB, E]), ALU.is_equal))
                    o.need()
                    gate_k = gates[:, :, k:k + 1].broadcast_to([P, TB, E])
                    if k == 0:
                        o.did(dve.tensor_copy(member[:, :, :], hit[:, :, :]))
                        o.did(dve.tensor_tensor(gate[:, :, :], hit[:, :, :], gate_k, ALU.mult))
                    else:
                        o.did(dve.tensor_tensor(member[:, :, :], member[:, :, :], hit[:, :, :], ALU.add))
                        o.need()
                        o.did(dve.tensor_tensor(hit[:, :, :], hit[:, :, :], gate_k, ALU.mult))
                        o.need()
                        o.did(dve.tensor_tensor(gate[:, :, :], gate[:, :, :], hit[:, :, :], ALU.add))
                o.need()
                dve.sem_inc(member_ready, 1)
                for c in range(3):
                    o.need()
                    o.did(dve.tensor_copy(r.gate[:, :, c, :], gate[:, :, :]))
                    if c < 2:
                        o.need()
                        o.did(dve.tensor_tensor(gate[:, :, :], gate[:, :, :], r.gate[:, :, c, :], ALU.subtract))
                o.did(dve.memset(off[:, 0, :], 0.0))
                dve.wait_ge(rank_mm, 1)
                for b in range(TB):
                    o.need()
                    o.did(dve.tensor_tensor(off[:, b + 1, :], off[:, b, :], ps[:, 1, b * E:(b + 1) * E], ALU.add))
                counts = off[:, TB, :]
                o.need()
                o.did(dve.tensor_tensor(r.slot[:, :, :], ps[:, 0, 0:TB * E].rearrange("p (b e) -> p b e", e=E),
                                        off[:, 0:TB, :], ALU.add))
                o.did(dve.tensor_scalar(blocks[:, :], counts, 0.0, None, ALU.is_gt))
                for m in range(1, -(-S // SLOTS)):
                    o.need()
                    o.did(dve.scalar_tensor_tensor(blocks[:, :], counts, float(m * SLOTS), blocks[:, :], ALU.is_gt, ALU.add))
                o.need()
                o.did(dve.tensor_tensor_scan(ends[:, :], ones_e[:, :], blocks[:, :], 0.0, ALU.mult, ALU.add))
                o.need()
                o.did(dve.tensor_tensor(starts[:, :], ends[:, :], blocks[:, :], ALU.subtract))
                o.need()
                o.did(dve.tensor_scalar(prod[:, :], starts[:, :], float(SLOTS), 1.0, ALU.mult, ALU.add))
                o.need()
                o.did(dve.tensor_tensor(r.slot[:, :, :], r.slot[:, :, :], repeat(prod[:, :], TB), ALU.add))
                o.need()
                o.did(dve.tensor_tensor(r.slot[:, :, :], r.slot[:, :, :], member[:, :, :], ALU.mult))
                o.need()
                o.did(dve.tensor_scalar(r.slot[:, :, :], r.slot[:, :, :], -1.0, None, ALU.add))
                o.did(dve.tensor_scalar(hit_e[:, :], ends[:, :], small[:, 0:1], None, ALU.is_le))
                o.need()
                o.did(dve.reduce_sum(item[:, 0:1], hit_e[:, :], axis=AX))
                o.need()
                o.did(dve.tensor_scalar(hit_e[:, :], iota_e[:, :], item[:, 0:1], None, ALU.is_equal))
                o.need()
                o.did(dve.tensor_tensor(prod[:, :], hit_e[:, :], counts, ALU.mult))
                o.need()
                o.did(dve.reduce_sum(item[:, 1:2], prod[:, :], axis=AX))
                o.need()
                o.did(dve.tensor_tensor(prod[:, :], hit_e[:, :], starts[:, :], ALU.mult))
                o.need()
                o.did(dve.reduce_sum(item[:, 2:3], prod[:, :], axis=AX))
                o.need()
                o.did(dve.tensor_tensor(item[:, 3:4], item[:, 2:3], small[:, 0:1], ALU.subtract))
                o.need()
                o.did(dve.scalar_tensor_tensor(item[:, 4:5], item[:, 3:4], float(SLOTS), item[:, 1:2], ALU.mult, ALU.add))
                o.need()
                o.did(dve.tensor_scalar(item[:, 5:6], item[:, 4:5], 0.0, None, ALU.is_gt))
                o.did(dve.tensor_scalar(above[:, :], steps[:, :], item[:, 4:5], None, ALU.is_lt))
                o.need()
                o.did(dve.reduce_sum(item[:, 7:8], above[:, :], axis=AX))
                o.need()
                o.did(dve.tensor_tensor(item[:, 5:6], item[:, 5:6], item[:, 7:8], ALU.add))
                o.need()
                o.did(dve.tensor_scalar(item[:, 6:7], item[:, 0:1], float(E - 1), None, ALU.min))
                o.need()
                o.did(dve.tensor_copy(meta_i[:, 0:1], item[:, 5:6]))
                o.did(dve.tensor_copy(meta_i[:, 1:2], item[:, 6:7]))
                o.did(dve.tensor_copy(meta_i[:, 2:3], ends[:, E - 1:E]))
                o.need()
                dve.sem_inc(meta_ready, 1)
                dve.wait_ge(bias_mm, 1)
                o.did(dve.tensor_copy(r.bias[:, 0:2].rearrange("p i m e -> p (i m e)"), ps[:, 2, :]))
                o.did(dve.tensor_copy(r.bias[:, 2].rearrange("p m e -> p (m e)"), ps[:, 3, 0:KC * E]))
                o.need()


def experts(nc, d, keep, rows, r):
    with ExitStack() as ctx:
        sb = lambda name, shape, dt=F32: ctx.enter_context(nc.sbuf_tensor(name, shape, dt))
        sem = lambda name: ctx.enter_context(nc.semaphore(name))
        ps = ctx.enter_context(nc.psum_tensor("ps_experts", [P, 8, HALF], F32))
        w = [sb(f"w_tile{g}", [P, KC, HALF]) for g in range(GROUPS)]
        onehot = sb("onehot", [P, TB, SLOTS], BF16)
        slot_col = sb("slot_col", [P, TB])
        tab_next, tab_now, tab_last = (sb(n, [P, 4], I32) for n in ("tab_next", "tab_now", "tab_last"))
        found, idx_f = sb("found", [P, 2, 6]), sb("idx_f", [P, 4, 2])
        bias = sb("bias_now", [P, 3, KC])
        xg = sb("xg", [P, 2, D])
        xT = sb("xT", [P, KC, SLOTS])
        gt, ut, sg = (sb(n, [P, 4, SLOTS]) for n in ("gt", "ut", "sg"))
        aT = sb("aT", [P, KC, SLOTS])
        yT = sb("yT", [P, KC, SLOTS])
        y = sb("y", [P, 2, D])
        pair = [ps[:, 2 * i:2 * i + 2, :].rearrange("p a (b n) -> p (a b) n", n=SLOTS) for i in range(3)]
        PAIR = (0, 1, 2, 0, 2, 1)
        side = 6

        def pair_free_at(j, g):
            before = [h for h in range(-GROUPS, g) if PAIR[h % GROUPS] == PAIR[g]][-1]
            return j * GROUPS + before + 4

        def turn_bank(q):
            return ps[:, (side, side + 1, 2, 3)[q], :].rearrange("p (a n) -> p a n", a=2)

        w_ready = [sem(f"w_ready{g}") for g in range(GROUPS)]
        onehot_ready, idx_mm, idx_ready = sem("onehot_ready"), sem("idx_mm"), sem("idx_ready")
        gathered, scattered, rows_out = sem("gathered"), sem("scattered"), sem("rows_out")
        xT_mm, xT_ready, group_done, pair_free = sem("xT_mm"), sem("xT_ready"), sem("group_done"), sem("pair_free")
        g_ready, sg_ready, a_ready = sem("g_ready"), sem("sg_ready"), sem("a_ready")
        back_mm, y_ready, tab_ready, order_s, passed = sem("back_mm"), sem("y_ready"), sem("tab_ready"), sem("order_e"), sem("passed")

        def level(eng, n):
            return eng.value_load(r.meta[0:1, 0, bass.ds(n, 1)] if not isinstance(n, int) else r.meta[0:1, 0, n:n + 1],
                                  min_val=0, max_val=len(LEVELS))

        def levels(eng, j):
            return nc.values_load_multi_w_load_instructions(r.meta[0:1, 0, bass.ds(j, 3)], [eng.engine], min_val=0,
                                                            max_val=len(LEVELS))[1]

        def expert(eng, n):
            return eng.value_load(r.meta[0:1, 1, bass.ds(n, 1)] if not isinstance(n, int) else r.meta[0:1, 1, n:n + 1],
                                  min_val=0, max_val=E - 1)

        def at_level(eng, lv, body, lo=1, hi=len(LEVELS)):
            if lo == hi:
                body(LEVELS[lo - 1])
                return
            mid = (lo + hi) // 2
            with eng.If(lv > mid):
                at_level(eng, lv, body, mid + 1, hi)
            with eng.Else():
                at_level(eng, lv, body, lo, mid)

        def halves(eng, lv, body):
            with eng.If(lv > ONE_HALF):
                body(2)
            with eng.Else():
                body(1)

        def rounds(eng, body):
            last = eng.value_load(r.meta[0:1, 2, 1:2], min_val=1, max_val=ITEMS)
            with eng.Fori(0, ITEMS + 1) as j:
                with eng.If(j <= last):
                    body(j)
                    eng.sem_inc(passed, 1)

        def hold(eng, s, value):
            eng.wait_ge(s, value)
            eng.sem_inc(passed, 1)

        sources = [(d["w_gate"], 0), (d["w_up"], 0), (d["w_gate"], 1), (d["w_up"], 1), (d["w_down"], 0), (d["w_down"], 1)]

        with nc.Block() as block:

            @block.sync
            def _(sp):
                def load(e, g):
                    src, c = sources[g]
                    at = src[0, bass.ds(e, 1), :, c * HALF:(c + 1) * HALF].rearrange("o (k p) n -> p (o k) n", p=P)
                    sp.dma_start(w[g][:, :, :], at).then_inc(w_ready[g], 16)

                e0 = expert(sp, 1)
                for g in range(GROUPS):
                    if g == 1:
                        sp.wait_ge(gathered, 32)
                    load(e0, g)

                def body(j):
                    lv, e = level(sp, j + 2), expert(sp, j + 2)
                    with sp.If(lv > 0):
                        for g in range(GROUPS):
                            sp.wait_ge(group_done, j * GROUPS + g + 1)
                            load(e, g)
                rounds(sp, body)

            @block.gpsimd
            def _(pool):
                def gather(j, n_halves):
                    for h in range(n_halves):
                        pool.indirect_dma_start(out=xg[:, h, :], out_offset=None, in_=rows.h2[:, :],
                                                in_offset=bass.IndirectOffsetOnAxis(ap=tab_next[:, h:h + 1].bitcast(U32), axis=0)
                                                ).then_inc(gathered, 32 // n_halves)

                def scatter(j, n_halves):
                    for h in range(n_halves):
                        hold(pool, y_ready, j * 2 + h + 1)
                        pool.indirect_dma_start(out=rows.x1[:, :],
                                                out_offset=bass.IndirectOffsetOnAxis(ap=tab_last[:, h:h + 1].bitcast(U32), axis=0),
                                                in_=y[:, h, :], in_offset=None, compute_op=ALU.add
                                                ).then_inc(scattered, 32 // n_halves)

                pool.sem_inc(rows_out, 1)
                hold(pool, idx_ready, 1)
                halves(pool, level(pool, 1), lambda nh: gather(-1, nh))

                def body(j):
                    last_lv, next_lv = level(pool, j), level(pool, j + 2)
                    with pool.If(next_lv > 0):
                        hold(pool, idx_ready, j + 2)
                        hold(pool, xT_mm, j * 4 + 4)
                        halves(pool, next_lv, lambda nh: gather(j, nh))
                    with pool.If(last_lv > 0):
                        hold(pool, tab_ready, j + 1)
                        halves(pool, last_lv, lambda nh: scatter(j, nh))
                        hold(pool, scattered, j * 32)
                    pool.sem_inc(rows_out, 1)
                rounds(pool, body)

            @block.scalar
            def _(act):
                act.sem_inc(y_ready, 2)

                def turn_in(j, nh):
                    for q in range(4):
                        act.wait_ge(xT_mm, (j + 1) * 4 + q + 1)
                        act.copy(xT[:, 2 * q:2 * q + 2, 0:nh * P], turn_bank(q)[:, :, 0:nh * P]).then_inc(xT_ready, 1)

                def sigmoid(j, nh, c):
                    act.wait_ge(g_ready, j * 2 + c + 1)
                    act.activation(sg[:, :, 0:nh * P], gt[:, :, 0:nh * P], ACT.Sigmoid, scale=ALPHA).then_inc(sg_ready, 1)

                def back(j, h, count):
                    act.wait_ge(tab_ready, j + 1)
                    act.wait_ge(back_mm, j * 2 + h + 1)
                    act.wait_ge(rows_out, j + 1)
                    act.activation(y[:, h, :].rearrange("p (a n) -> p a n", a=2), ps[:, side:side + 2, :], ACT.Copy,
                                   scale=tab_last[:, 2 + h:3 + h].bitcast(F32)).then_inc(y_ready, count)

                halves(act, level(act, 1), lambda nh: turn_in(-1, nh))

                def body(j):
                    last_lv, lv, next_lv = levels(act, j)
                    with act.If(lv > 0):
                        halves(act, lv, lambda nh: sigmoid(j, nh, 0))
                    with act.If(last_lv > 0):
                        with act.If(last_lv > ONE_HALF):
                            back(j, 0, 1)
                        with act.Else():
                            back(j, 0, 2)
                    with act.If(lv > 0):
                        halves(act, lv, lambda nh: sigmoid(j, nh, 1))
                    with act.If(last_lv > ONE_HALF):
                        back(j, 1, 1)
                    with act.If(next_lv > 0):
                        halves(act, next_lv, lambda nh: turn_in(j, nh))
                rounds(act, body)

            @block.vector
            def _(dve):
                dve.sem_inc(pair_free, 3)
                STEPS = 3 + 11 + 6 + 2 + 2
                o = Order(dve, order_s)

                def match(j):
                    e = expert(dve, j + 2)
                    o.did(dve.tensor_copy(slot_col[:, :], r.slot[:, :, bass.ds(e, 1)].rearrange("p b o -> p (b o)")))
                    o.did(dve.tensor_copy(r.tok_gate[:, :, 2:5], r.gate[:, :, :, bass.ds(e, 1)].rearrange("p b c o -> p b (c o)")))
                    step = 0.0 if isinstance(j, int) else float(SLOTS)
                    o.did(dve.tensor_scalar(r.iota[:, :], r.iota[:, :], step, None, ALU.add))
                    o.need()
                    for b in range(TB):
                        o.did(dve.tensor_scalar(onehot[:, b, :], r.iota[:, :], slot_col[:, b:b + 1], None, ALU.is_equal))
                    o.need()
                    dve.sem_inc(onehot_ready, 1)

                def table(j):
                    token, empty, gate_sum = idx_f[:, 0], idx_f[:, 1], idx_f[:, 2]
                    dve.wait_ge(idx_mm, j + 2)
                    o.did(dve.tensor_copy(found[:, :, :].rearrange("p h c -> p (h c)"), ps[:, side, 0:12]))
                    o.need()
                    o.did(dve.tensor_tensor(token, found[:, :, 0], found[:, :, 1], ALU.add))
                    o.did(dve.tensor_tensor(gate_sum, found[:, :, 2], found[:, :, 3], ALU.add))
                    o.need()
                    o.did(dve.tensor_scalar(empty, token, 0.0, None, ALU.is_equal))
                    o.did(dve.tensor_tensor(tab_next[:, 2:4].bitcast(F32), gate_sum, found[:, :, 4], ALU.add))
                    o.need()
                    o.did(dve.tensor_tensor(empty, empty, r.pad[:, :], ALU.mult))
                    o.need()
                    dve.scalar_tensor_tensor(tab_next[:, 0:2], empty, -1.0, token, ALU.add, ALU.add).then_inc(idx_ready, 1)
                    hold(dve, idx_ready, j + 2)

                def gate_in(j, n, c):
                    dve.wait_ge(group_done, j * GROUPS + 2 * c + 1)
                    dve.tensor_tensor(gt[:, :, 0:n], pair[PAIR[2 * c]][:, :, 0:n], bcast(bias[:, 0, 4 * c:4 * c + 4], n),
                                      ALU.add).then_inc(pair_free, 1)
                    dve.wait_ge(pair_free, j * GROUPS + 2 * c + 4)
                    dve.tensor_scalar(gt[:, :, 0:n], gt[:, :, 0:n], LIMIT, None, ALU.min).then_inc(g_ready, 1)

                def up_in(j, n, c):
                    dve.wait_ge(sg_ready, j * 2 + c + 1)
                    o.did(dve.tensor_tensor(sg[:, :, 0:n], gt[:, :, 0:n], sg[:, :, 0:n], ALU.mult))
                    dve.wait_ge(group_done, j * GROUPS + 2 * c + 2)
                    dve.tensor_tensor(ut[:, :, 0:n], pair[PAIR[2 * c + 1]][:, :, 0:n], bcast(bias[:, 1, 4 * c:4 * c + 4], n),
                                      ALU.add).then_inc(pair_free, 1)
                    dve.wait_ge(pair_free, j * GROUPS + 2 * c + 5)
                    o.did(dve.tensor_scalar(ut[:, :, 0:n], ut[:, :, 0:n], LIMIT, -LIMIT, ALU.min, ALU.max))
                    o.need()
                    dve.scalar_tensor_tensor(aT[:, 4 * c:4 * c + 4, 0:n], ut[:, :, 0:n], 1.0, sg[:, :, 0:n], ALU.add,
                                             ALU.mult).then_inc(a_ready, 1)

                def down_in(j, n, c):
                    dve.wait_ge(group_done, j * GROUPS + c + 5)
                    dve.tensor_tensor(yT[:, 4 * c:4 * c + 4, 0:n], pair[PAIR[4 + c]][:, :, 0:n], bcast(bias[:, 2, 4 * c:4 * c + 4], n),
                                      ALU.add).then_inc(pair_free, 1)

                match(-1)
                table(-1)
                o.did(dve.memset(gt[:, :, :], 0.0))
                o.did(dve.memset(yT[:, :, :], 0.0))
                o.did(dve.memset(tab_now[:, :], 0))
                o.need()
                first_steps = o.n

                def body(j):
                    lv, next_lv = level(dve, j + 1), level(dve, j + 2)
                    e = expert(dve, j + 1)

                    def restart(at):
                        o.base, o.n = j * STEPS + first_steps, at

                    restart(0)
                    dve.wait_ge(rows_out, j + 1)
                    o.did(dve.tensor_copy(tab_last[:, :], tab_now[:, :]))
                    o.need()
                    o.did(dve.tensor_copy(tab_now[:, :], tab_next[:, :]))
                    o.did(dve.tensor_copy(bias[:, :, :].rearrange("p i m -> p (i m)"),
                                          r.bias[:, :, :, bass.ds(e, 1)].rearrange("p i m o -> p (i m o)")))
                    o.need()
                    dve.sem_inc(tab_ready, 1)
                    with dve.If(next_lv > 0):
                        match(j)
                        table(j)
                    with dve.Else():
                        dve.sem_inc(order_s, 11 + 6)

                    def item(n):
                        restart(3 + 11 + 6)
                        for c in range(2):
                            gate_in(j, n, c)
                            up_in(j, n, c)
                        for c in range(2):
                            down_in(j, n, c)
                        assert o.n == STEPS
                    with dve.If(lv > 0):
                        at_level(dve, lv, item)
                rounds(dve, body)

            @block.tensor
            def _(pe):
                def product(j, g, n, rhs):
                    order = [(m, k) for m in range(4) for k in range(KC)]
                    if g == 4:
                        order = [(m, k) for k0 in (0, KC // 2) for m in (0, 2) for k in range(k0, k0 + KC // 2)] + order[KC:2 * KC] + order[3 * KC:]
                        pe.wait_ge(a_ready, j * 2 + 1)
                    pe.wait_ge(w_ready[g], j * 16 + 16)
                    pe.wait_ge(pair_free, pair_free_at(j, g))
                    for i, (m, k) in enumerate(order):
                        if g == 4 and i == KC:
                            pe.wait_ge(a_ready, j * 2 + 2)
                        ins = pe.matmul(pair[PAIR[g]][:, m, 0:n], w[g][:, k, m * P:(m + 1) * P], rhs[:, k, 0:n],
                                        start=k == 0, stop=k == KC - 1)
                    ins.then_inc(group_done, 1)

                def index(j):
                    pe.wait_ge(onehot_ready, j + 2)
                    for h in range(2):
                        for b in range(TB):
                            ins = pe.matmul(ps[:, side, 6 * h:6 * h + 6], onehot[:, b, h * P:(h + 1) * P], r.tok_gate[:, b, :],
                                            start=b == 0, stop=b == TB - 1)
                    ins.then_inc(idx_mm, 1)

                def turn_in(j, nh):
                    hold(pe, gathered, (j + 2) * 32)
                    if isinstance(j, int):
                        hold(pe, idx_ready, j + 2)
                    else:
                        hold(pe, y_ready, j * 2 + 2)
                        hold(pe, pair_free, j * GROUPS + 5)
                    for q in range(4):
                        for a in range(2):
                            for h in range(nh):
                                k = 2 * q + a
                                ins = pe.transpose(turn_bank(q)[:, a, h * P:(h + 1) * P], xg[:, h, k * P:(k + 1) * P],
                                                   keep.ident[:, :])
                        ins.then_inc(xT_mm, 1)

                def back(j, h, count):
                    for k in range(KC):
                        ins = pe.transpose(ps[:, side + k // 4, (k % 4) * P:(k % 4 + 1) * P], yT[:, k, h * P:(h + 1) * P],
                                           keep.ident[:, :])
                    ins.then_inc(back_mm, count)

                def back_first(j, last_lv, next_lv):
                    with pe.If(last_lv > 0):
                        hold(pe, pair_free, j * GROUPS + 3)
                        hold(pe, y_ready, j * 2)
                        with pe.If(next_lv > 0):
                            hold(pe, idx_ready, j + 2)
                        with pe.If(last_lv > ONE_HALF):
                            back(j, 0, 1)
                        with pe.Else():
                            back(j, 0, 2)

                def back_second(j, last_lv):
                    with pe.If(last_lv > ONE_HALF):
                        hold(pe, y_ready, j * 2 + 1)
                        back(j, 1, 1)

                pe.sem_inc(back_mm, 2)
                index(-1)
                halves(pe, level(pe, 1), lambda nh: turn_in(-1, nh))

                def body(j):
                    last_lv, lv, next_lv = levels(pe, j)

                    def item(n):
                        pe.wait_ge(xT_ready, j * 4 + 4)
                        product(j, 0, n, xT)
                        with pe.If(next_lv > 0):
                            index(j)
                        product(j, 1, n, xT)
                        back_first(j, last_lv, next_lv)
                        product(j, 2, n, xT)
                        back_second(j, last_lv)
                        product(j, 3, n, xT)
                        with pe.If(next_lv > 0):
                            halves(pe, next_lv, lambda nh: turn_in(j, nh))
                        product(j, 4, n, aT)
                        with pe.If(next_lv > 0):
                            hold(pe, xT_ready, j * 4 + 8)
                        product(j, 5, n, aT)
                    with pe.If(lv > 0):
                        at_level(pe, lv, item)
                    with pe.Else():
                        back_first(j, last_lv, next_lv)
                        back_second(j, last_lv)
                rounds(pe, body)


def final(nc, d, keep, rows, out):
    with ExitStack() as ctx:
        sb = lambda name, shape, dt=F32: ctx.enter_context(nc.sbuf_tensor(name, shape, dt))
        sem = lambda name: ctx.enter_context(nc.semaphore(name))
        x2, y2, g = sb("x2", [P, TB, D]), sb("y2", [P, TB, D]), sb("g_final", [P, D])
        junk, ss, rstd, tmp = sb("junk_f", [P, D]), sb("ss_f", [P, TB]), sb("rstd_f", [P, TB]), sb("tmp_f", [P, 3, TB])
        x_in, st = [sem(f"xf_in{b}") for b in range(TB)], [sem(f"out_st{b}") for b in range(TB)]
        g_in, squares, ready, normed, order_s = sem("gf_in"), sem("squares_f"), sem("ready_f"), sem("normed_f"), sem("order_f")
        with nc.Block() as block:

            @block.sync
            def _(sp):
                for b in range(TB):
                    sp.dma_start(x2[:, b, :], rows.x1[b * P:(b + 1) * P, :]).then_inc(x_in[b], 16)
                for b in range(TB):
                    sp.wait_ge(ready, b + 1)
                    sp.dma_start(out[0, b * P:(b + 1) * P, :], y2[:, b, :]).then_inc(st[b], 16)
                for b in range(TB):
                    sp.wait_ge(st[b], 16)

            @block.scalar
            def _(act):
                act.dma_start(g[:, :], d["final_g"].partition_broadcast(P)).then_inc(g_in, 16)
                for b in range(TB):
                    act.wait_ge(x_in[b], 16)
                    if b:
                        act.wait_ge(squares, b)
                    act.activation(junk[:, :], x2[:, b, :], ACT.Square, accum_out=ss[:, b:b + 1]).then_inc(squares, 1)

            @block.vector
            def _(dve):
                dve.wait_ge(g_in, 16)
                for b in range(TB):
                    dve.wait_ge(normed, b // 2 + 1)
                    dve.scalar_tensor_tensor(y2[:, b, :], x2[:, b, :], rstd[:, b:b + 1], g[:, :], ALU.mult,
                                             ALU.mult).then_inc(ready, 1)

            @block.gpsimd
            def _(pool):
                o = Order(pool, order_s)
                for pair in range(TB // 2):
                    pool.wait_ge(squares, 2 * (pair + 1))
                    c = slice(2 * pair, 2 * pair + 2)
                    rsqrt_mean(pool, o, rstd[:, c], ss[:, c], tmp[:, :, c], D)
                    o.need()
                    pool.sem_inc(normed, 1)


class Rows:

    def __init__(self, nc):
        self.x1 = nc.dram_tensor("x1_rows", (ROWS, D), F32, kind="Internal").ap()
        self.h2 = nc.dram_tensor("h2_rows", (ROWS, D), F32, kind="Internal").ap()
        self.meta = nc.dram_tensor("meta_rows", (3, P), I32, kind="Internal").ap()


class Kept:

    def __init__(self, sb):
        self.ident = sb("ident", [P, P])
        self.logits = sb("logits", [P, TB, E])


class Routes:

    def __init__(self, sb):
        self.slot = sb("slot", [P, TB, E])
        self.gate = sb("gate", [P, TB, 3, E], BF16)
        self.bias = sb("bias", [P, 3, KC, E])
        self.iota = sb("iota_slots", [P, SLOTS])
        self.pad = sb("pad_rows", [P, 2])
        self.tok_gate = sb("tok_gate", [P, TB, 6], BF16)
        self.meta = sb("meta", [1, 3, P + 1], I32)


def build(nc, d, out):
    rows = Rows(nc)
    with ExitStack() as ctx:
        sb = lambda name, shape, dt=F32: ctx.enter_context(nc.sbuf_tensor(name, shape, dt))
        keep = Kept(sb)
        mixer(nc, d, keep, rows)
        r = Routes(sb)
        routing(nc, d, keep, rows, r)
        experts(nc, d, keep, rows, r)
        final(nc, d, keep, rows, out)


INPUTS = ["x", "norm1_g", "w_in", "lambda_q1", "lambda_k1", "lambda_q2", "lambda_k2", "subln_g", "w_pool", "b_pool",
          "pool_scale", "w_out", "norm2_g", "router_w", "router_b", "w_gate", "b_gate", "w_up", "b_up", "w_down",
          "b_down", "final_g"]


def kernel(**inputs):
    import concourse.bacc as bacc
    from concourse.bass_utils import run_bass_kernel_spmd

    nc = bacc.Bacc("TRN2", target_bir_lowering=False, num_devices=1)
    arrays, d = {}, {}
    for name in INPUTS:
        a = np.ascontiguousarray(inputs[name])
        arrays["in_" + name] = a
        d[name] = nc.dram_tensor("in_" + name, a.shape, mybir.dt.from_np(a.dtype), kind="ExternalInput").ap()
    out = nc.dram_tensor("out", (1, S, D), F32, kind="ExternalOutput").ap()
    build(nc, d, out)
    r = run_bass_kernel_spmd(nc, [arrays], core_ids=[0])
    return r.results[0]["out"]
```
